# Optimizing a Trainium2 kernel written in Bass

```python
import jax, jax.numpy as jnp
from jax import lax
import numpy as np

D_MODEL = 2048
BATCH = 1
SEQ = 256
DEPTH = 1

CHUNK = 64
HEAD_DIM = 64
N_HEADS_SWA = 16
N_KV_SWA = 4
N_HEADS_FOX = 16
WINDOW = 128
WINDOW_CHUNKS = WINDOW // CHUNK
Q_BLOCK = 128
ROPE_THETA = 10000.0
D_FF = 5632
CONV_W = 3
EPS = 1e-5
NEG_INF = -1e30

MIX_WIDTH = (N_HEADS_SWA + N_HEADS_FOX) * HEAD_DIM
SWA_Q = N_HEADS_SWA * HEAD_DIM
SWA_KV = N_KV_SWA * HEAD_DIM
FOX_W = N_HEADS_FOX * HEAD_DIM
IN_SPLITS = (SWA_Q, SWA_KV, SWA_KV, FOX_W, FOX_W, FOX_W, N_HEADS_FOX)
IN_WIDTH = SWA_Q + 2 * SWA_KV + 3 * FOX_W + N_HEADS_FOX

kernel_name = "hymba_swa_sink_fox_convffn"

def rms_norm(x, g):
    xf = x.astype(jnp.float32)
    y = xf * lax.rsqrt(jnp.mean(xf * xf, axis=-1, keepdims=True) + EPS)
    return (y * g.astype(jnp.float32)).astype(x.dtype)

def rope(x, pos):
    half = HEAD_DIM // 2
    inv_freq = 1.0 / (ROPE_THETA ** (jnp.arange(half, dtype=jnp.float32) * (2.0 / HEAD_DIM)))
    ang = pos.astype(jnp.float32)[:, None] * inv_freq[None, :]
    cos = jnp.cos(ang)[None, :, None, :]
    sin = jnp.sin(ang)[None, :, None, :]
    xf = x.astype(jnp.float32)
    x1, x2 = xf[..., :half], xf[..., half:]
    out = jnp.concatenate([x1 * cos - x2 * sin, x2 * cos + x1 * sin], axis=-1)
    return out.astype(x.dtype)

def swa_sink_attention(q, k, v, sinks):
    B, S = q.shape[0], q.shape[1]
    NC = S // CHUNK
    G = N_HEADS_SWA // N_KV_SWA
    qc = q.reshape(B, NC, CHUNK, N_KV_SWA, G, HEAD_DIM)
    kc = k.reshape(B, NC, CHUNK, N_KV_SWA, HEAD_DIM)
    vc = v.reshape(B, NC, CHUNK, N_KV_SWA, HEAD_DIM)

    def shift_chunks(a, j):
        return jnp.pad(a, ((0, 0), (j, 0), (0, 0), (0, 0), (0, 0)))[:, :NC]

    shifts = list(range(WINDOW_CHUNKS - 1, -1, -1))
    kb = jnp.concatenate([shift_chunks(kc, j) for j in shifts], axis=2)
    vb = jnp.concatenate([shift_chunks(vc, j) for j in shifts], axis=2)
    key_shift = jnp.asarray(np.repeat(np.array(shifts), CHUNK))
    valid = jnp.arange(NC)[:, None] >= key_shift[None, :]

    scale = 1.0 / float(np.sqrt(HEAD_DIM))
    s = jnp.einsum('bnqhgd,bnkhd->bnhgqk', qc, kb).astype(jnp.float32) * scale
    s = jnp.where(valid[None, :, None, None, None, :], s, NEG_INF)
    sink = sinks.astype(jnp.float32).reshape(N_KV_SWA, G)[None, None, :, :, None, None]
    m = jnp.maximum(jnp.max(s, axis=-1, keepdims=True), sink)
    p = jnp.exp(s - m)
    denom = jnp.sum(p, axis=-1, keepdims=True) + jnp.exp(sink - m)
    w = (p / denom).astype(v.dtype)
    o = jnp.einsum('bnhgqk,bnkhd->bnqhgd', w, vb)
    return o.reshape(B, S, N_HEADS_SWA * HEAD_DIM)

def forgetting_attention(q, k, v, log_f):
    B, S = q.shape[0], q.shape[1]
    NB = S // Q_BLOCK
    F = jnp.cumsum(log_f, axis=1).transpose(0, 2, 1)
    kt = k.transpose(0, 2, 1, 3)
    vt = v.transpose(0, 2, 1, 3)
    qb = q.reshape(B, NB, Q_BLOCK, N_HEADS_FOX, HEAD_DIM).transpose(1, 0, 3, 2, 4)
    Fq = F.reshape(B, N_HEADS_FOX, NB, Q_BLOCK).transpose(2, 0, 1, 3)
    key_pos = jnp.arange(S)
    scale = 1.0 / float(np.sqrt(HEAD_DIM))

    def block(args):
        qi, Fqi, i = args
        s = jnp.einsum('bhqd,bhkd->bhqk', qi, kt).astype(jnp.float32) * scale
        s = s + Fqi[..., None] - F[:, :, None, :]
        qpos = i * Q_BLOCK + jnp.arange(Q_BLOCK)
        mask = key_pos[None, :] <= qpos[:, None]
        s = jnp.where(mask[None, None], s, NEG_INF)
        p = jax.nn.softmax(s, axis=-1).astype(vt.dtype)
        return jnp.einsum('bhqk,bhkd->bhqd', p, vt)

    out = lax.map(block, (qb, Fq, jnp.arange(NB)))
    return out.transpose(1, 0, 3, 2, 4).reshape(B, S, N_HEADS_FOX * HEAD_DIM)

def conv_gated_ffn(h, w_up, conv_w, conv_b, w_down):
    S = h.shape[1]
    u = h @ w_up
    up = jnp.pad(u, ((0, 0), (CONV_W - 1, 0), (0, 0)))
    c = conv_b + sum(up[:, j:j + S] * conv_w[j] for j in range(CONV_W))
    gate, val = c[..., :D_FF], c[..., D_FF:]
    return (jax.nn.silu(gate) * val) @ w_down

def setup_inputs(seed: int = 0) -> dict:
    key = jax.random.key(seed)
    ks = jax.random.split(key, 14)
    f32 = jnp.float32
    x = jax.random.normal(ks[0], (BATCH, SEQ, D_MODEL), f32)
    norm_mix = 1.0 + 0.02 * jax.random.normal(ks[1], (DEPTH, D_MODEL), f32)
    w_in = jax.random.normal(ks[2], (DEPTH, D_MODEL, IN_WIDTH), f32) * D_MODEL ** -0.5
    sinks = 0.5 * jax.random.normal(ks[3], (DEPTH, N_HEADS_SWA), f32)
    b_f = jax.random.uniform(ks[4], (DEPTH, N_HEADS_FOX), f32, 1.0, 5.0)
    w_o = jax.random.normal(ks[5], (DEPTH, MIX_WIDTH, D_MODEL), f32) * MIX_WIDTH ** -0.5
    norm_ffn = 1.0 + 0.02 * jax.random.normal(ks[6], (DEPTH, D_MODEL), f32)
    w_up = jax.random.normal(ks[7], (DEPTH, D_MODEL, 2 * D_FF), f32) * D_MODEL ** -0.5
    conv_w = jax.random.normal(ks[8], (DEPTH, CONV_W, 2 * D_FF), f32) * CONV_W ** -0.5
    conv_b = 0.01 * jax.random.normal(ks[9], (DEPTH, 2 * D_FF), f32)
    w_down = jax.random.normal(ks[10], (DEPTH, D_FF, D_MODEL), f32) * D_FF ** -0.5
    norm_final = 1.0 + 0.02 * jax.random.normal(ks[11], (D_MODEL,), f32)
    return {"x": x, "norm_mix": norm_mix, "w_in": w_in, "sinks": sinks, "b_f": b_f,
            "w_o": w_o, "norm_ffn": norm_ffn, "w_up": w_up, "conv_w": conv_w,
            "conv_b": conv_b, "w_down": w_down, "norm_final": norm_final}

def reference(x, norm_mix, w_in, sinks, b_f, w_o, norm_ffn, w_up, conv_w, conv_b, w_down, norm_final):
    B, S = x.shape[0], x.shape[1]
    pos = jnp.arange(S)
    split_at = [int(v) for v in np.cumsum(IN_SPLITS)[:-1]]
    for l in range(DEPTH):
        h = rms_norm(x, norm_mix[l])
        proj = h @ w_in[l]
        qa, ka, va, qf, kf, vf, f_logit = jnp.split(proj, split_at, axis=-1)
        qa = rope(qa.reshape(B, S, N_HEADS_SWA, HEAD_DIM), pos)
        ka = rope(ka.reshape(B, S, N_KV_SWA, HEAD_DIM), pos)
        va = va.reshape(B, S, N_KV_SWA, HEAD_DIM)
        out_a = swa_sink_attention(qa, ka, va, sinks[l])
        qf = qf.reshape(B, S, N_HEADS_FOX, HEAD_DIM)
        kf = kf.reshape(B, S, N_HEADS_FOX, HEAD_DIM)
        vf = vf.reshape(B, S, N_HEADS_FOX, HEAD_DIM)
        log_f = jax.nn.log_sigmoid(f_logit.astype(jnp.float32) + b_f[l].astype(jnp.float32))
        out_b = forgetting_attention(qf, kf, vf, log_f)
        mixed = jnp.concatenate([out_a, out_b], axis=-1)
        x = x + mixed @ w_o[l]
        h = rms_norm(x, norm_ffn[l])
        x = x + conv_gated_ffn(h, w_up[l], conv_w[l], conv_b[l], w_down[l])
    return rms_norm(x, norm_final)


_drawn_inputs = setup_inputs


def setup_inputs(seed=0):
    import zlib

    import numpy as np

    out = dict(_drawn_inputs(seed))
    spreads = {}
    factors = {'norm_mix': 5.78, 'sinks': 8.0, 'norm_ffn': 3.85, 'conv_b': 8.0, 'norm_final': 2.909}
    for name, (base, spread) in spreads.items():
        noise = np.random.default_rng([zlib.crc32(name.encode()), seed]).standard_normal(out[name].shape)
        drawn = base * np.exp(spread * noise) if base else spread * noise
        out[name] = __import__('jax').numpy.asarray(drawn.astype(out[name].dtype))
    for name, factor in factors.items():
        out[name] = (out[name] * factor).astype(out[name].dtype)
    return out
```

```python
import numpy as np
import concourse.bass as bass
from concourse import mybir
from contextlib import ExitStack

F32 = mybir.dt.float32
R32 = mybir.dt.float32r
ALU = mybir.AluOpType
ACT = mybir.ActivationFunctionType
AX = mybir.AxisListType

P = 128
D = 2048
S = 256
KB = D // P
MT = S // P
HD = 64
NKV = 4
NH = 16
F = 5632
FB = F // P
EPS = 1e-5
QSCALE = HD ** -0.5
COL_QA, COL_KA, COL_VA = 0, 1024, 1280
COL_QF, COL_KF, COL_VF, COL_F = 1536, 2560, 3584, 4608

RING = 4
WARM = 9
LEAD = 3
TILE = 1024
VA_COLS = 256 + NH
SLOT = 4 * VA_COLS
QUADS = 4
UP_STEPS = FB // 2
QUAD_STEPS = 13
UP_DVE_STEPS = 4
GROUPS = D // 512
DOWN_TILES = FB // 2

T_KA = 4
T_QUAD = 8
QUAD_TILES = 16
T_WOA = T_QUAD + QUADS * QUAD_TILES
WOA_UNITS = 3
T_WOB = T_WOA + 4 * WOA_UNITS
WO_UNITS = 8
T_UP = T_WOB + 4 * (WO_UNITS - WOA_UNITS)
UP_TILES = 8
T_DOWN = T_UP + UP_STEPS * UP_TILES
HALF = 768
T_END = T_DOWN + GROUPS * DOWN_TILES
WOA_ORDER = [(u, kt) for kt in (0, 2, 1, 3) for u in range(WOA_UNITS)]

SLOTS_LOOP = {0: ["S0"], 2: ["S1"], 3: ["T0"], 4: ["S2", "V0"], 5: ["T1"], 6: ["S3", "V1"], 7: ["T2"],
              8: ["V2"], 9: ["T3"], 10: ["V3"]}
SLOTS_TAIL = {0: ["S0"], 1: ["S1"], 2: ["S2"], 3: ["T0", "S3"], 4: ["V0", "T1"], 5: ["V1", "T2"],
              6: ["V2", "T3"], 7: ["V3"]}


def at_slot(slots, s, kind):
    return [int(e[1]) for e in slots.get(s, []) if e[0] == kind]


class Steps:

    def __init__(self, eng, sem):
        self.eng, self.sem, self.base, self.k, self.i, self.per = eng, sem, 0, 0, 0, 0

    def loop(self, i, first, per):
        self.base, self.k = self.base + self.k - first * per, 0
        self.i, self.per = i, per

    def end(self, passes_end):
        assert self.k == self.per, f"steps per pass: {self.k}"
        self.base, self.k, self.i, self.per = self.base + passes_end * self.per, 0, 0, 0

    def done(self, ins):
        ins.then_inc(self.sem, 1)
        self.k += 1

    def wait(self):
        self.eng.wait_ge(self.sem, self.i * self.per + (self.base + self.k))


class Sbuf:

    def __init__(self, nc):
        self.nc, self.cursor = nc, (nc.sbuf_base + 63) // 64 * 64

    def place(self, name, shape, dt=F32):
        t = self.nc.alloc_sbuf_tensor_at(name, shape, dt, offset=self.cursor)
        self.cursor += (4 * int(np.prod(shape[1:])) + 31) // 32 * 32
        return t


def program(nc, x, norm_mix, w_in, sinks, b_f, w_o, norm_ffn, w_up, conv_w, conv_b, w_down, norm_final,
            ident_c, tri_c, mask_a_c, mask_b_c, cos_c, sin_c, out):
    ctx = ExitStack()
    with ctx:
        sbuf = Sbuf(nc)
        sb = sbuf.place

        def ps(name, shape):
            return ctx.enter_context(nc.psum_tensor(name, shape, F32))

        def sem(name):
            return ctx.enter_context(nc.semaphore(name))

        raw = sb("raw", [P, RING, SLOT])
        hi = sb("hi", [P, RING, SLOT], R32)
        lo = sb("lo", [P, RING, SLOT], R32)
        nat = sb("nat", [P, MT, D])
        act_hi = sb("act_hi", [P, KB, S], R32)
        act_lo_at = sbuf.cursor
        act_lo = sb("act_lo", [P, KB, S], R32)
        ident = sb("ident", [P, P])
        ones = sb("ones", [P, P])
        cst = sb("cst", [P, 384])
        r2b = sb("r2b", [P, S])
        small = sb("small", [P, 96])

        region = sbuf.cursor
        g_hi = sb("g_hi", [P, FB, S], R32)
        g_lo = sb("g_lo", [P, FB, S], R32)
        region_end = sbuf.cursor
        sbuf.cursor = region
        mix_hi = sb("mix_hi", [P, KB, S], R32)
        mix_lo = sb("mix_lo", [P, KB, S], R32)
        va = sb("va", [P, MT, S])
        kta = sb("kta", [P, NKV, S])
        kq = sb("kq", [P, S])
        vq = sb("vq", [P, MT, HD])
        qa = sb("qa", [P, 2, S])
        kf = sb("kf", [P, 2, S])
        qf = sb("qf", [P, 2, S])
        vf = sb("vf", [P, MT, S])
        prob = sb("prob", [P, 4, 2, 384])
        prob_t = sb("prob_t", [P, 2, 2, 384])
        cos_r = sb("cos_r", [P, S])
        sin_r = sb("sin_r", [P, S])
        cos_t = sb("cos_t", [P, S])
        sin_t = sb("sin_t", [P, S])
        swap = sb("swap", [P, 2, S])
        rope_a = sb("rope_a", [P, 2, S])
        rope_b = sb("rope_b", [P, 2, S])
        r1b = sb("r1b", [P, S])
        diag = sb("diag", [P, MT, P])
        mask_a = sb("mask_a", [P, 384])
        mask_b = sb("mask_b", [P, 384])
        tri_f = sb("tri_f", [P, S])
        tri = sb("tri", [P, S], R32)
        fg = sb("fg", [P, 8, MT, NH])
        nlf_hi = sb("nlf_hi", [P, MT, NH], R32)
        nlf_lo = sb("nlf_lo", [P, MT, NH], R32)
        nlfq = sb("nlfq", [P, 2, MT, 4], R32)
        fcum = sb("fcum", [P, MT, NH])
        fq = sb("fq", [P, MT, 4])
        nsink = sb("nsink", [P, MT, NH])
        nsq = sb("nsq", [P, MT, 4])
        stat = sb("stat", [P, 4, 5, 4])
        bf_b = sb("bf_b", [P, NH])

        assert sbuf.cursor <= region_end
        sbuf.cursor = region_end
        ub = sb("ub", [P, 2, 2, S + 2])
        conv_o = sb("conv_o", [P, 2, 2, S])
        silu = sb("silu", [P, 2, S])
        top = sbuf.cursor
        sbuf.cursor = region_end
        xts = sb("xts", [P, 2, S])
        yt = sb("yt", [P, 2, 2, S])
        ysq = sb("ysq", [P, 2, S])
        ysum = sb("ysum", [P, 2, S])
        xcols = sb("xcols", [P, MT, 2 * P])
        assert max(top, sbuf.cursor) <= nc.sbuf_usable_end
        sbuf.cursor = act_lo_at
        gfin = sb("gfin", [P, D])
        sq_out = sb("sq_out", [P, MT, 512])

        acc = [ps(f"acc{i}", [P, 512]) for i in range(3)]
        sc_ps = ps("sc_ps", [P, 2, 512])
        tr_ps = ps("tr_ps", [P, 2, 512])
        pv_ps = ps("pv_ps", [P, 512])
        x_banks = [acc[0][:], acc[2][:], acc[1][:], sc_ps[:, 0], sc_ps[:, 1], tr_ps[:, 0], tr_ps[:, 1], pv_ps[:]]

        d_w = [sem(f"d_w{i}") for i in range(RING)]
        d_x = [sem(f"d_x{i}") for i in range(4)]
        d_id, d_nrm, d_cnv, d_cst, d_gf, d_out = (sem(n) for n in (
            "d_id", "d_nrm", "d_cnv", "d_cst", "d_gf", "d_out"))
        hi_done, lo_done, mm_done = sem("hi_done"), sem("lo_done"), sem("mm_done")
        act_step, dve_step, pool_step = sem("act_step"), sem("dve_step"), sem("pool_step")
        cst_t, cst_c = sem("cst_t"), sem("cst_c")
        x_t, xhi, xlo = sem("x_t"), sem("xhi"), sem("xlo")
        evac_d, evac_a = sem("evac_d"), sem("evac_a")
        ones_s = sem("ones_s")
        rms1_root, rms1_done, diag_done, rms1_ps, r1b_done = (sem(n) for n in (
            "rms1_root", "rms1_done", "diag_done", "rms1_ps", "r1b_done"))
        f_abs, f_ln, nlf_s, fcum_ps, fcum_s = (sem(n) for n in (
            "f_abs", "f_ln", "nlf_s", "fcum_ps", "fcum_s"))
        tri_s, kta_s, swap_s, krope_s, nsink_s, quad_s = (sem(n) for n in (
            "tri_s", "kta_s", "swap_s", "krope_s", "nsink_s", "quad_s"))
        scores_s, read_s, negmax_s, exp_s, prob_s, pt_ps, pt_s, pv_s, mixhi_s, mixlo_s = (sem(n) for n in (
            "scores_s", "read_s", "negmax_s", "exp_s", "prob_s", "pt_ps", "pt_s", "pv_s", "mixhi_s", "mixlo_s"))
        xcols_s, xt_ps, xts_s, yt_s, ysq_s, yhi_s, ylo_s, yt_ps, ynat_s, ysum_s, y2_ps, y2_root, r2_s = (sem(n) for n in (
            "xcols_s", "xt_ps", "xts_s", "yt_s", "ysq_s", "yhi_s", "ylo_s", "yt_ps", "ynat_s", "ysum_s", "y2_ps",
            "y2_root", "r2_s"))
        pad_s, u_s, c0_s, conv_s, silu_s, gated_s, ghi_s, glo_s = (sem(n) for n in (
            "pad_s", "u_s", "c0_s", "conv_s", "silu_s", "gated_s", "ghi_s", "glo_s"))
        z_s, zsq_s, z_tot, z_root, z_rms, fin_a, fin_d = (sem(n) for n in (
            "z_s", "zsq_s", "z_tot", "z_root", "z_rms", "fin_a", "fin_d"))

        win = w_in[0].rearrange("(t c p) n -> t p c n", p=P, c=4)
        wo = w_o[0].rearrange("(t c p) n -> t p c n", p=P, c=4)
        wup = w_up[0].rearrange("(t c p) n -> t p c n", p=P, c=4)
        wdn = w_down[0].rearrange("(t c p) n -> t p c n", p=P, c=2)

        def narrow(t, slot):
            return t[:, slot, 0:TILE].rearrange("p (c n) -> p c n", c=4)

        def wide(t, slot):
            return t[:, slot, 0:TILE].rearrange("p (c n) -> p c n", c=2)

        def with_gates(t, slot):
            return t[:, slot].rearrange("p (c n) -> p c n", c=4)

        flat = prob[:].rearrange("p a b n -> p (a b n)")
        rows = flat[:, D:D + 5 * P].rearrange("p (j n) -> p j n", j=5)
        eps = small[:, 0:1]
        ss1 = small[:, 2:4]
        root1 = small[:, 4:6]
        r1c = small[:, 6:8]
        ss3 = small[:, 8:16].rearrange("p (m g) -> p m g", m=2)
        tot3 = small[:, 16:18]
        root3 = small[:, 18:20]
        r3 = small[:, 20:22]
        g1 = cst[:, 0:KB]
        g2 = cst[:, KB:2 * KB]

        def tap(j, b, n=1):
            return cst[:, bass.ds(32 + 88 * j + b, n)]

        block = ctx.enter_context(nc.Block())

        @block.sync
        def _(sp):
            sp.dma_start(rows[0:KB, 0], norm_mix.rearrange("a (b p) -> (a b) p", p=P)).then_inc(d_nrm, 16)
            for c in range(4):
                for m in range(MT):
                    sp.dma_start(nat[:, m, c * 512:(c + 1) * 512],
                                 x[0, m * P:(m + 1) * P, c * 512:(c + 1) * 512]).then_inc(d_x[c], 16)
                sp.dma_start(with_gates(raw, c)[:, :, 0:256], win[c][:, :, COL_VA:COL_VA + 256]).then_inc(d_w[c], 16)
                sp.dma_start(with_gates(raw, c)[:, :, 256:VA_COLS], win[c][:, :, COL_F:COL_F + NH]).then_inc(d_w[c], 16)

            def load(t, slot, dst, src):
                sp.wait_ge(lo_done, t - (RING - 1))
                sp.dma_start(dst, src).then_inc(d_w[slot], 16)

            def load_unit(t, w, col, kts=range(4)):
                for k, kt in enumerate(kts):
                    load(t + k, k, narrow(raw, k), w[kt][:, :, bass.ds(col, 256)])

            load_unit(T_KA, win, COL_KA)
            with sp.Fori(0, QUADS) as j:
                for n, col in enumerate((COL_QA, COL_KF, COL_QF, COL_VF)):
                    load_unit(j * QUAD_TILES + (T_QUAD + 4 * n), win, j * 256 + col)
            for n, (u, kt) in enumerate(WOA_ORDER):
                load(T_WOA + n, n % RING, narrow(raw, n % RING), wo[kt][:, :, u * 256:(u + 1) * 256])
            with sp.Fori(0, WO_UNITS - WOA_UNITS) as u:
                load_unit(u * 4 + T_WOB, wo, u * 256 + WOA_UNITS * 256)
            with sp.Fori(0, UP_STEPS) as i:
                load_unit(i * UP_TILES + T_UP, wup, i * 256)
                load_unit(i * UP_TILES + (T_UP + 4), wup, i * 256 + F)
            with sp.Fori(0, GROUPS // 2) as g:
                for k in range(2 * DOWN_TILES):
                    n, kt = divmod(k, DOWN_TILES)
                    load(g * (2 * DOWN_TILES) + (T_DOWN + k), k % RING, wide(raw, k % RING),
                         wdn[kt][:, :, bass.ds(g * 1024 + n * 512, 512)])
            for h in range(2):
                sp.wait_ge(fin_a, h + 1)
                sp.dma_start(out[0, 0:P, h * HALF:(h + 1) * HALF], nat[:, 0, h * HALF:(h + 1) * HALF]).then_inc(d_out, 16)
            sp.wait_ge(fin_d, 2)
            sp.dma_start(out[0, 0:P, 2 * HALF:D], nat[:, 0, 2 * HALF:D]).then_inc(d_out, 16)
            sp.wait_ge(d_out, 80)

        @block.gpsimd
        def _(pool):
            pool.memset(ones[:], 1.0).then_inc(ones_s, 1)
            for j in range(3):
                pool.dma_start(rows[0:2 * FB, 1 + j], conv_w[0, j].rearrange("(b p) -> b p", p=P)).then_inc(d_cnv, 16)
            pool.dma_start(rows[0:2 * FB, 4], conv_b.rearrange("a (b p) -> (a b) p", p=P)).then_inc(d_cnv, 16)
            for dst, src in ((cos_t[:], cos_c), (sin_t[:], sin_c), (tri_f[:], tri_c), (mask_a[:], mask_a_c),
                             (mask_b[:], mask_b_c), (nsink[:, 0], sinks[0].partition_broadcast(P)),
                             (nsink[:, 1], sinks[0].partition_broadcast(P)), (bf_b[:], b_f[0].partition_broadcast(P))):
                pool.dma_start(dst, src).then_inc(d_cst, 16)
            for c in range(4):
                pool.wait_ge(d_x[c], 32)
            pool.wait_ge(kta_s, 4)
            pool.wait_ge(evac_a, 1)
            pool.wait_ge(nlf_s, 2)
            pool.wait_ge(fcum_s, 1)
            pool.wait_ge(nsink_s, 1)
            with pool.Fori(0, QUADS) as j:
                pool.wait_ge(mixlo_s, j * 4 + 1)
                pool.tensor_copy(kq[:], kta[:, bass.ds(j, 1), :].rearrange("p a n -> p (a n)"))
                pool.tensor_copy(vq[:], va[:, :, bass.ds(j * HD, HD)])
                pool.tensor_copy(fq[:], fcum[:, :, bass.ds(j * 4, 4)])
                pool.tensor_copy(nsq[:], nsink[:, :, bass.ds(j * 4, 4)])
                pool.tensor_copy(nlfq[:, 0], nlf_hi[:, :, bass.ds(j * 4, 4)].bitcast(F32))
                pool.tensor_copy(nlfq[:, 1], nlf_lo[:, :, bass.ds(j * 4, 4)].bitcast(F32)).then_inc(quad_s, 1)
            pool.tensor_copy(xcols[:], nat[:, :, 0:2 * P]).then_inc(xcols_s, 1)
            with pool.Fori(1, WO_UNITS) as u:
                pool.wait_ge(xt_ps, u)
                pool.tensor_copy(xcols[:], nat[:, :, bass.ds(u * 2 * P, 2 * P)]).then_inc(xcols_s, 1)
            pool.wait_ge(mm_done, T_DOWN)
            pool.dma_start(gfin[:], norm_final.partition_broadcast(P)).then_inc(d_gf, 16)

        @block.scalar
        def _(act):
            act.dma_start(ident[:], ident_c).then_inc(d_id, 16)
            act.dma_start(rows[KB:2 * KB, 0], norm_ffn.rearrange("a (b p) -> (a b) p", p=P)).then_inc(d_nrm, 16)
            st = Steps(act, act_step)

            def split_hi(t, slot):
                act.wait_ge(d_w[slot], (t - slot) * (16 // RING) + 32)
                if not (isinstance(t, int) and t < RING):
                    act.wait_ge(mm_done, t - (RING - 1))
                n = SLOT if isinstance(t, int) and t < T_KA else TILE
                act.activation(hi[:, slot, 0:n], raw[:, slot, 0:n], ACT.Copy).then_inc(hi_done, 1)

            act.wait_ge(cst_t, 1)
            act.activation(cst[:, 0:2 * KB], pv_ps[:, 0:2 * KB], ACT.Copy).then_inc(cst_c, 1)
            act.wait_ge(cst_c, 1)
            for c in range(KB):
                act.wait_ge(x_t, c // 2 + 1)
                act.activation(act_hi[:, c], x_banks[c // 2][:, (c % 2) * S:(c % 2 + 1) * S], ACT.Copy,
                               scale=g1[:, c:c + 1]).then_inc(xhi, 1)
                if c % 4 == 3 and c // 4 < LEAD:
                    split_hi(c // 4, c // 4)

            def rope_swap(bank, scale):
                for o in range(0, P, 32):
                    i = o ^ 32
                    ins = act.activation(swap[o:o + 32].rearrange("p a n -> p (a n)"), bank[i:i + 32, :], ACT.Copy, scale=scale)
                ins.then_inc(swap_s, 1)

            def values(bank, dst):
                act.activation(dst[:, 0], bank[:, 0:S], ACT.Copy, scale=r1c[:, 0:1])
                act.activation(dst[:, 1], bank[:, S:2 * S], ACT.Copy, scale=r1c[:, 1:2]).then_inc(evac_a, 1)

            split_hi(3, 3)
            act.wait_ge(d_x[3], 32)
            for m in range(MT):
                split_hi(4 + m, m)
                if m > 0:
                    st.wait()
                st.done(act.activation(flat[:, 0:D], nat[:, m, :], ACT.Square, accum_out=ss1[:, m:m + 1]))
            act.wait_ge(pad_s, 1)
            st.wait()
            act.activation(root1, ss1, ACT.Sqrt, bias=eps, scale=1.0 / D).then_inc(rms1_root, 1)
            split_hi(6, 2)
            for s in range(4):
                split_hi(T_KA + s + LEAD, (s + LEAD) % RING)
                if s == 0:
                    act.wait_ge(rms1_done, 1)
                    act.wait_ge(mm_done, 4)
                    for m, bank in enumerate((acc[0], acc[2])):
                        ins = act.activation(va[:, m], bank[:, 0:256], ACT.Copy, scale=r1c[:, m:m + 1])
                    ins.then_inc(evac_a, 1)
                if s == 1:
                    act.wait_ge(f_abs, 1)
                    st.done(act.activation(fg[:, 2], fg[:, 1], ACT.Exp, scale=-1.0))
                    st.wait()
                    act.activation(fg[:, 3], fg[:, 2], ACT.Ln, bias=1.0).then_inc(f_ln, 1)
                if s == 2:
                    act.wait_ge(rms1_ps, 1)
                    act.activation(r1b[:], sc_ps[:, 0, 0:S], ACT.Copy).then_inc(r1b_done, 1)
                if s == 3:
                    act.wait_ge(mm_done, T_KA + 4)
                    rope_swap(acc[1], 1.0)
                    act.wait_ge(fcum_ps, 1)
                    act.activation(fcum[:].rearrange("p a n -> p (a n)"), pv_ps[:, 0:MT * NH], ACT.Copy,
                                   scale=-1.0).then_inc(fcum_s, 1)
                    act.wait_ge(cst_t, 2)
                    act.activation(cst[:, 2 * KB:384], pv_ps[:, 128:480], ACT.Copy).then_inc(cst_c, 1)
                    act.wait_ge(krope_s, 1)
                    for h in range(2):
                        for e in range(2):
                            act.activation(kta[h * 64:h * 64 + 64, e::2, :], rope_b[e * 64:e * 64 + 64],
                                           ACT.Copy).then_inc(kta_s, 1)

            def attention(s, slots, q):
                for p in at_slot(slots, s - 1, "S"):
                    act.wait_ge(negmax_s, q * 4 + (p + 1))
                    for t in range(2):
                        for h in range(2):
                            pr = prob[:, p, h, 0:128] if t == 0 else prob[:, p, h, 128:384]
                            ins = act.activation(pr, pr, ACT.Exp, bias=stat[:, p, 0, 2 * t + h:2 * t + h + 1],
                                                 accum_out=stat[:, p, 1, 2 * t + h:2 * t + h + 1])
                    if p < 2:
                        ins = act.activation(stat[:, p, 3], stat[:, p, 2], ACT.Exp)
                    ins.then_inc(exp_s, 1)
                for e in slots.get(s, []):
                    p = int(e[1])
                    if e[0] == "T":
                        act.wait_ge(pt_ps, q * 4 + (p + 1))
                        act.activation(prob_t[:, p % 2], tr_ps[:, :, 0:384], ACT.Copy).then_inc(pt_s, 1)
                    if e[0] == "V":
                        act.wait_ge(pv_s, q * 4 + (p + 1))
                        chunk = q * 2 + (p if p < 2 else 8 + p - 2)
                        act.activation(mix_hi[:, bass.ds(chunk, 1), :].rearrange("p a n -> p (a n)"), pv_ps[:, 0:S],
                                       ACT.Copy).then_inc(mixhi_s, 1)

            def quad(j, attend):
                for s in range(QUAD_TILES):
                    split_hi(j * QUAD_TILES + (T_QUAD + s + LEAD), (s + LEAD) % RING)
                    if s in (3, 15):
                        act.wait_ge(mm_done, j * QUAD_TILES + (T_QUAD + s + 1))
                        if s == 3:
                            act.wait_ge(krope_s, j + 1)
                            rope_swap(acc[0], QSCALE)
                        else:
                            values(acc[1], vf)
                    if attend:
                        attention(s, SLOTS_LOOP, j - 1)

            quad(0, False)
            with act.Fori(1, QUADS) as j:
                quad(j, True)

            def take_xt(u):
                act.wait_ge(xt_ps, u + 1)
                if not (isinstance(u, int) and u == 0):
                    act.wait_ge(yt_s, u)
                act.activation(xts[:].rearrange("p a n -> p (a n)"), sc_ps[:, 0], ACT.Copy).then_inc(xts_s, 1)

            def after_y(u, par):
                act.wait_ge(yt_s, u + 1)
                if not (isinstance(u, int) and u == 0):
                    act.wait_ge(ysum_s, u)
                act.activation(ysq[:], yt[:, par], ACT.Square).then_inc(ysq_s, 1)
                for b in range(2):
                    act.activation(act_hi[:, bass.ds(u * 2 + b, 1), :].rearrange("p a n -> p (a n)"), yt[:, par, b],
                                   ACT.Copy, scale=cst[:, bass.ds(u * 2 + (KB + b), 1)]).then_inc(yhi_s, 1)

            def take_ynat(u):
                act.wait_ge(yt_ps, u + 1)
                act.activation(nat[:, :, bass.ds(u * 256, 256)], sc_ps[:, 1].rearrange("p (m n) -> p m n", m=2),
                               ACT.Copy).then_inc(ynat_s, 1)

            for s in range(4 * WOA_UNITS):
                split_hi(T_WOA + s + LEAD, (s + LEAD) % RING)
                attention(s, SLOTS_TAIL, QUADS - 1)
                if s >= 8 and s < 11:
                    take_xt(s - 8)
                if s >= 10:
                    take_ynat(s - 10)
                if s >= 9:
                    after_y(s - 9, (s - 9) % 2)

            def wo_unit(u, par):
                t = u * 4 + (T_WOB - 4 * WOA_UNITS)
                for s in range(4):
                    split_hi(t + (s + LEAD), (s + LEAD) % RING)
                    if s == 0:
                        take_ynat(u - 1)
                    if s == 2:
                        take_xt(u)
                    if s == 3:
                        after_y(u, par)

            wo_unit(WOA_UNITS, WOA_UNITS % 2)
            with act.Fori(0, 2) as i:
                wo_unit(i * 2 + 4, 0)
                wo_unit(i * 2 + 5, 1)

            def up_step(i, first):
                for s in range(UP_TILES):
                    split_hi(i * UP_TILES + (T_UP + s + LEAD), (s + LEAD) % RING)
                    if first and s == 0:
                        take_ynat(WO_UNITS - 1)
                    if first and s == 1:
                        act.wait_ge(y2_ps, 1)
                        act.activation(ysq[:, 0], pv_ps[:, 0:S], ACT.Sqrt, bias=eps, scale=1.0 / D).then_inc(y2_root, 1)
                    if s in (3, 7):
                        v = s // 4
                        for b in range(2):
                            act.wait_ge(u_s, i * 4 + (2 * v + b + 1))
                            act.activation(conv_o[:, v, b], ub[:, v, b, 2:S + 2], ACT.Identity,
                                           scale=tap(2, i * 2 + (b + v * FB)), bias=tap(3, i * 2 + (b + v * FB))).then_inc(c0_s, 1)
                    if s == 5:
                        act.wait_ge(conv_s, i * 4 + 2)
                        if not first:
                            act.wait_ge(glo_s, i)
                        act.activation(silu[:], conv_o[:, 0], ACT.Silu).then_inc(silu_s, 1)
                    if s == 7:
                        for b in range(2):
                            act.wait_ge(gated_s, i * 2 + (b + 1))
                            act.activation(g_hi[:, bass.ds(i * 2 + b, 1), :].rearrange("p a n -> p (a n)"), silu[:, b],
                                           ACT.Copy).then_inc(ghi_s, 1)

            up_step(0, True)
            with act.Fori(1, UP_STEPS) as i:
                up_step(i, False)

            def squares(n):
                if n > 0:
                    act.wait_ge(zsq_s, n)
                for m in range(MT):
                    act.wait_ge(z_s, 2 * n + (m + 5))
                    ins = act.activation(sq_out[:, m], nat[:, m, n * 512:(n + 1) * 512], ACT.Square,
                                         accum_out=ss3[:, m, n:n + 1])
                ins.then_inc(zsq_s, 1)

            act.activation(small[:, 24:25], eps, ACT.Sqrt)
            for t in range(GROUPS * DOWN_TILES):
                if T_DOWN + t + LEAD < T_END:
                    split_hi(T_DOWN + t + LEAD, (t + LEAD) % RING)
                if t % DOWN_TILES == DOWN_TILES - 1:
                    squares(t // DOWN_TILES)
            act.wait_ge(z_tot, 1)
            act.activation(root3, tot3, ACT.Sqrt, bias=eps, scale=1.0 / D).then_inc(z_root, 1)
            act.wait_ge(z_rms, GROUPS)
            for h in range(2):
                act.activation(nat[:, 0, h * HALF:(h + 1) * HALF], nat[:, 0, h * HALF:(h + 1) * HALF], ACT.Copy,
                               scale=r3[:, 0:1]).then_inc(fin_a, 1)
            for h in range(2):
                act.wait_ge(fin_d, 2 * h + 1)
                c0, c1 = (0, 2 * HALF) if h == 0 else (2 * HALF, D)
                act.dma_start(out[0, P:2 * P, c0:c1], nat[:, 1, c0:c1]).then_inc(d_out, 16)

        @block.vector
        def _(dve):
            st = Steps(dve, dve_step)

            def split_lo(t, slot):
                dve.wait_ge(hi_done, t + 1)
                n = SLOT if isinstance(t, int) and t < T_KA else TILE
                dve.tensor_tensor(lo[:, slot, 0:n], raw[:, slot, 0:n], hi[:, slot, 0:n].bitcast(F32),
                                  ALU.subtract).then_inc(lo_done, 1)

            dve.memset(small[:, 90:91], 0.0).then_inc(read_s, 1)
            dve.memset(small[:, 91:92], 0.0).then_inc(mixlo_s, 1)
            dve.memset(small[:, 92:93], 0.0).then_inc(z_s, 4)
            dve.memset(eps, EPS).then_inc(pad_s, 1)
            dve.wait_ge(cst_c, 1)
            for c in range(KB):
                dve.wait_ge(xhi, c // 2 * 2 + 2)
                dve.scalar_tensor_tensor(act_lo[:, c], x_banks[c // 2][:, (c % 2) * S:(c % 2 + 1) * S], g1[:, c:c + 1],
                                         act_hi[:, c].bitcast(F32), ALU.mult, ALU.subtract).then_inc(xlo, 1)
                if c % 4 == 3 and c // 4 < LEAD:
                    split_lo(c // 4, c // 4)
            split_lo(3, 3)
            dve.wait_ge(d_cst, 128)
            dve.tensor_scalar(nsink[:], nsink[:], -1.0, None, ALU.mult).then_inc(nsink_s, 1)
            dve.tensor_copy(tri[:], tri_f[:]).then_inc(tri_s, 1)
            split_lo(4, 0)
            split_lo(5, 1)
            dve.wait_ge(rms1_root, 1)
            dve.reciprocal(r1c, root1).then_inc(rms1_done, 1)
            dve.wait_ge(rms1_done, 1)
            dve.wait_ge(d_id, 16)
            for m in range(MT):
                dve.tensor_scalar(diag[:, m], ident[:], r1c[:, m:m + 1], None, ALU.mult).then_inc(diag_done, 1)
            split_lo(6, 2)

            def rope(bank, scale, tmp):
                dve.scalar_tensor_tensor(tmp[:], bank[:].rearrange("p (a n) -> p a n", a=2), scale,
                                         cos_r[:].unsqueeze(1).broadcast_to([P, 2, S]), ALU.mult, ALU.mult).then_inc(evac_d, 1)

            def rope_rest(dst, tmp):
                st.done(dve.tensor_tensor(swap[:], swap[:], sin_r[:].unsqueeze(1).broadcast_to([P, 2, S]), ALU.mult))
                st.wait()
                return dve.tensor_tensor(dst[:], tmp[:], swap[:], ALU.add)

            for s in range(4):
                split_lo(T_KA + s + LEAD, (s + LEAD) % RING)
                if s == 1:
                    dve.wait_ge(evac_a, 1)
                    for m, bank in enumerate((acc[0], acc[2])):
                        st.done(dve.scalar_tensor_tensor(fg[:, 0, m], bank[:, 256:VA_COLS], r1c[:, m:m + 1],
                                                         bf_b[:], ALU.mult, ALU.add))
                    st.wait()
                    dve.scalar_tensor_tensor(fg[:, 1], fg[:, 0], -1.0, fg[:, 0], ALU.mult, ALU.max).then_inc(f_abs, 1)
                    st.done(dve.tensor_scalar(fg[:, 4], fg[:, 0], 0.0, None, ALU.min))
                    dve.wait_ge(f_ln, 1)
                    st.wait()
                    st.done(dve.tensor_tensor(fg[:, 5], fg[:, 3], fg[:, 4], ALU.subtract))
                    st.wait()
                    dve.tensor_copy(nlf_hi[:], fg[:, 5]).then_inc(nlf_s, 1)
                    dve.wait_ge(nlf_s, 1)
                    dve.tensor_tensor(nlf_lo[:], fg[:, 5], nlf_hi[:].bitcast(F32), ALU.subtract).then_inc(nlf_s, 1)
                if s == 2:
                    dve.wait_ge(r1b_done, 1)
                    st.done(dve.tensor_tensor(cos_r[:], cos_t[:], r1b[:], ALU.mult))
                    st.done(dve.tensor_tensor(sin_r[:], sin_t[:], r1b[:], ALU.mult))
                    st.wait()
                if s == 3:
                    dve.wait_ge(mm_done, T_KA + 4)
                    dve.wait_ge(swap_s, 1)
                    rope(acc[1], 1.0, rope_a)
                    dve.wait_ge(evac_d, 1)
                    rope_rest(rope_b, rope_a).then_inc(krope_s, 1)

            def attention(s, slots, q):
                for p in at_slot(slots, s - 2, "S"):
                    dve.wait_ge(exp_s, q * 4 + (p + 1))
                    if p < 2:
                        st.done(dve.tensor_tensor(stat[:, p, 1], stat[:, p, 1], stat[:, p, 3], ALU.add))
                        st.wait()
                    st.done(dve.reciprocal(stat[:, p, 4], stat[:, p, 1]))
                    st.wait()
                    for t in range(2):
                        for h in range(2):
                            pr = prob[:, p, h, 0:128] if t == 0 else prob[:, p, h, 128:384]
                            ins = dve.tensor_scalar(pr, pr, stat[:, p, 4, 2 * t + h:2 * t + h + 1], None, ALU.mult)
                    ins.then_inc(prob_s, 1)
                for e in slots.get(s, []):
                    p = int(e[1])
                    if e[0] == "S":
                        dve.wait_ge(scores_s, q * 4 + (p + 1))
                        if p < 2:
                            ins = dve.tensor_tensor(prob[:, p], sc_ps[:, :, 0:384],
                                                    mask_a[:].unsqueeze(1).broadcast_to([P, 2, 384]), ALU.add)
                        else:
                            for t in range(2):
                                for h in range(2):
                                    c0, c1 = (0, 128) if t == 0 else (128, 384)
                                    i = (p - 2) * 2 + h
                                    ins = dve.scalar_tensor_tensor(prob[:, p, h, c0:c1], sc_ps[:, h, c0:c1],
                                                                   fq[:, t, i:i + 1], mask_b[:, c0:c1], ALU.add, ALU.add)
                        ins.then_inc(read_s, 1)
                        dve.wait_ge(read_s, q * 4 + (p + 2))
                        for t in range(2):
                            c0, c1 = (0, 128) if t == 0 else (128, 384)
                            ins = dve.tensor_reduce(stat[:, p, 0, 2 * t:2 * t + 2], prob[:, p, :, c0:c1], AX.X, ALU.max,
                                                    negate=True)
                            if p < 2:
                                st.done(ins)
                        if p < 2:
                            st.wait()
                            nsv = nsq[:, :, 2 * p:2 * p + 2]
                            mv = stat[:, p, 0].rearrange("p (t h) -> p t h", t=2)
                            st.done(dve.tensor_tensor(mv, mv, nsv, ALU.min))
                            st.wait()
                            ins = dve.tensor_tensor(stat[:, p, 2].rearrange("p (t h) -> p t h", t=2), mv, nsv, ALU.subtract)
                        ins.then_inc(negmax_s, 1)
                    if e[0] == "V":
                        dve.wait_ge(mixhi_s, q * 4 + (p + 1))
                        chunk = q * 2 + (p if p < 2 else 8 + p - 2)
                        mh = mix_hi[:, bass.ds(chunk, 1), :].rearrange("p a n -> p (a n)").bitcast(F32)
                        dve.tensor_tensor(mix_lo[:, bass.ds(chunk, 1), :].rearrange("p a n -> p (a n)"), pv_ps[:, 0:S], mh,
                                          ALU.subtract).then_inc(mixlo_s, 1)

            def quad(j, attend):
                for s in range(QUAD_TILES):
                    split_lo(j * QUAD_TILES + (T_QUAD + s + LEAD), (s + LEAD) % RING)
                    if s == 3:
                        dve.wait_ge(mm_done, j * QUAD_TILES + (T_QUAD + 4))
                        dve.wait_ge(swap_s, j + 2)
                        rope(acc[0], QSCALE, rope_a)
                        dve.wait_ge(evac_d, j * 3 + 2)
                        rope_rest(qa, rope_a).then_inc(krope_s, 1)
                    if s in (7, 11):
                        dve.wait_ge(mm_done, j * QUAD_TILES + (T_QUAD + s + 1))
                        bank, dst, scale = (acc[1], kf, 1.0) if s == 7 else (acc[0], qf, QSCALE)
                        dve.scalar_tensor_tensor(dst[:], bank[:].rearrange("p (a n) -> p a n", a=2), scale,
                                                 r1b[:].unsqueeze(1).broadcast_to([P, 2, S]), ALU.mult,
                                                 ALU.mult).then_inc(evac_d, 1)
                    if attend:
                        if s == 0:
                            dve.wait_ge(quad_s, j)
                        attention(s, SLOTS_LOOP, j - 1)

            quad(0, False)
            with dve.Fori(1, QUADS) as j:
                st.loop(j, 1, QUAD_STEPS)
                quad(j, True)
                st.end(QUADS)

            def make_y(u, par, bank):
                dve.wait_ge(xts_s, u + 1)
                if not (isinstance(u, int) and u < 2):
                    dve.wait_ge(yt_ps, u - 1)
                dve.tensor_tensor(yt[:, par].rearrange("p a n -> p (a n)"), bank[:], xts[:].rearrange("p a n -> p (a n)"),
                                  ALU.add).then_inc(yt_s, 1)
                dve.wait_ge(yt_s, u + 1)
                dve.wait_ge(ysq_s, u + 1)
                if not (isinstance(u, int) and u == 0):
                    dve.wait_ge(ysum_s, u)
                dve.tensor_tensor(ysum[:], ysum[:], ysq[:], ALU.add).then_inc(ysum_s, 1)
                for b in range(2):
                    dve.wait_ge(yhi_s, u * 2 + (b + 1))
                    ins = dve.scalar_tensor_tensor(
                        act_lo[:, bass.ds(u * 2 + b, 1), :].rearrange("p a n -> p (a n)"), yt[:, par, b],
                        cst[:, bass.ds(u * 2 + (KB + b), 1)],
                        act_hi[:, bass.ds(u * 2 + b, 1), :].rearrange("p a n -> p (a n)").bitcast(F32),
                        ALU.mult, ALU.subtract)
                ins.then_inc(ylo_s, 1)

            st.done(dve.memset(ysum[:], 0.0))
            for s in range(4 * WOA_UNITS):
                split_lo(T_WOA + s + LEAD, (s + LEAD) % RING)
                if s == 0:
                    dve.wait_ge(quad_s, QUADS)
                attention(s, SLOTS_TAIL, QUADS - 1)
                if s >= 9:
                    dve.wait_ge(mm_done, T_WOA + s + 1)
                    if s == 9:
                        st.wait()
                    make_y(s - 9, (s - 9) % 2, acc[s - 9])

            def wo_unit(u, par, bank):
                t = u * 4 + (T_WOB - 4 * WOA_UNITS)
                for s in range(4):
                    split_lo(t + (s + LEAD), (s + LEAD) % RING)
                dve.wait_ge(mm_done, t + 4)
                make_y(u, par, bank)

            wo_unit(WOA_UNITS, WOA_UNITS % 2, acc[0])
            with dve.Fori(0, 2) as i:
                wo_unit(i * 2 + 4, 0, acc[1])
                wo_unit(i * 2 + 5, 1, acc[0])

            def up_step(i, first):
                if not first:
                    st.loop(i, 1, UP_DVE_STEPS)
                for s in range(UP_TILES):
                    split_lo(i * UP_TILES + (T_UP + s + LEAD), (s + LEAD) % RING)
                    if first and s == 1:
                        dve.wait_ge(y2_root, 1)
                        dve.reciprocal(r2b[:], ysq[:, 0]).then_inc(r2_s, 1)
                        dve.wait_ge(r2_s, 1)
                    if first and s == 2:
                        st.done(dve.memset(ub[:, :, :, 0:2], 0.0))
                        st.wait()
                    if s in (3, 7):
                        v = s // 4
                        bank = acc[2] if v == 0 else acc[1]
                        dve.wait_ge(mm_done, i * UP_TILES + (T_UP + s + 1))
                        for b in range(2):
                            dve.tensor_tensor(ub[:, v, b, 2:S + 2], bank[:, b * S:(b + 1) * S], r2b[:],
                                              ALU.mult).then_inc(u_s, 1)
                        for b in range(2):
                            dve.wait_ge(c0_s, i * 4 + (2 * v + b + 1))
                            st.done(dve.scalar_tensor_tensor(conv_o[:, v, b], ub[:, v, b, 1:S + 1],
                                                             tap(1, i * 2 + (b + v * FB)), conv_o[:, v, b],
                                                             ALU.mult, ALU.add))
                        for b in range(2):
                            if b == 0:
                                st.wait()
                            dve.scalar_tensor_tensor(conv_o[:, v, b], ub[:, v, b, 0:S], tap(0, i * 2 + (b + v * FB)),
                                                     conv_o[:, v, b], ALU.mult, ALU.add).then_inc(conv_s, 1)
                    if s == 7:
                        dve.wait_ge(silu_s, i + 1)
                        for b in range(2):
                            dve.wait_ge(conv_s, i * 4 + (b + 3))
                            dve.tensor_tensor(silu[:, b], silu[:, b], conv_o[:, 1, b], ALU.mult).then_inc(gated_s, 1)
                        for b in range(2):
                            dve.wait_ge(ghi_s, i * 2 + (b + 1))
                            ins = dve.tensor_tensor(g_lo[:, bass.ds(i * 2 + b, 1), :].rearrange("p a n -> p (a n)"),
                                                    silu[:, b],
                                                    g_hi[:, bass.ds(i * 2 + b, 1), :].rearrange("p a n -> p (a n)").bitcast(F32),
                                                    ALU.subtract)
                        ins.then_inc(glo_s, 1)
                if not first:
                    st.end(UP_STEPS)

            up_step(0, True)
            with dve.Fori(1, UP_STEPS) as i:
                up_step(i, False)

            def make_z(n):
                bank = sc_ps if n % 2 == 0 else tr_ps
                for m in range(MT):
                    dve.tensor_tensor(nat[:, m, n * 512:(n + 1) * 512], bank[:, m],
                                      nat[:, m, n * 512:(n + 1) * 512], ALU.add).then_inc(z_s, 1)

            def gain(n):
                dve.wait_ge(zsq_s, n + 1)
                for m in range(MT):
                    ins = dve.tensor_tensor(nat[:, m, n * 512:(n + 1) * 512], nat[:, m, n * 512:(n + 1) * 512],
                                            gfin[:, n * 512:(n + 1) * 512], ALU.mult)
                ins.then_inc(z_rms, 1)

            for t in range(GROUPS * DOWN_TILES):
                if T_DOWN + t + LEAD < T_END:
                    split_lo(T_DOWN + t + LEAD, (t + LEAD) % RING)
                n, kt = divmod(t, DOWN_TILES)
                if t == 0:
                    dve.wait_ge(ynat_s, WO_UNITS)
                if kt == DOWN_TILES - 1:
                    dve.wait_ge(mm_done, T_DOWN + t + 1)
                    make_z(n)
                if kt == 4 and n > 0:
                    if n == 1:
                        dve.wait_ge(d_gf, 16)
                    gain(n - 1)
            dve.wait_ge(zsq_s, GROUPS)
            dve.tensor_reduce(tot3, ss3, AX.X, ALU.add).then_inc(z_tot, 1)
            dve.wait_ge(z_root, 1)
            dve.reciprocal(r3, root3).then_inc(z_rms, 1)
            dve.wait_ge(z_rms, GROUPS)
            dve.tensor_scalar(nat[:, 1, 0:2 * HALF], nat[:, 1, 0:2 * HALF], r3[:, 1:2], None, ALU.mult).then_inc(fin_d, 1)
            for m in range(MT):
                dve.scalar_tensor_tensor(nat[:, m, 2 * HALF:D], nat[:, m, 2 * HALF:D], r3[:, m:m + 1],
                                         gfin[:, 2 * HALF:D], ALU.mult, ALU.mult).then_inc(fin_d, 1)

        @block.tensor
        def _(pe):
            pe.wait_ge(ones_s, 1)
            for n in range(WARM):
                pe.matmul(tr_ps[:, 0, 0:P], ones[:], ones[:], start=True, stop=True)
            pe.wait_ge(d_id, 16)
            pe.wait_ge(d_nrm, 32)
            pe.transpose(pv_ps[:, 0:2 * KB], rows[0:2 * KB, 0, :], ident[0:2 * KB, 0:2 * KB]).then_inc(cst_t, 1)

            def turn_x_pair(pr):
                pe.wait_ge(d_x[pr // 2], 32)
                if pr == 7:
                    pe.wait_ge(cst_c, 1)
                for b in range(2):
                    for m in range(MT):
                        o = b * S + m * P
                        c = 2 * pr + b
                        ins = pe.transpose(x_banks[pr][:, o:o + P], nat[:, m, c * P:(c + 1) * P], ident[:])
                ins.then_inc(x_t, 1)

            for pr in range(4):
                turn_x_pair(pr)

            def mm3(dst, a_hi, a_lo, b_hi, b_lo, start=False):
                pe.matmul(dst, a_hi, b_hi, start=start, stop=False, skip_group_check=True)
                pe.matmul(dst, a_hi, b_lo, start=False, stop=False, skip_group_check=True)
                return pe.matmul(dst, a_lo, b_hi, start=False, stop=True, skip_group_check=True)

            def features(t, slot, bank, kt, a_hi, a_lo, first):
                pe.wait_ge(lo_done, t + 1)
                wh, wl = narrow(hi, slot), narrow(lo, slot)
                for c in range(4):
                    for b in range(2):
                        ins = mm3(bank[:, b * S:(b + 1) * S], wh[:, c, b * P:(b + 1) * P], wl[:, c, b * P:(b + 1) * P],
                                  a_hi[:, 4 * kt + c], a_lo[:, 4 * kt + c], start=first and c == 0 and b == 0)
                ins.then_inc(mm_done, 1)

            def tokens(t, slot, bank, kt, first):
                pe.wait_ge(lo_done, t + 1)
                wh, wl = narrow(hi, slot), narrow(lo, slot)
                for c in range(4):
                    for m in range(MT):
                        k = 4 * kt + c
                        ins = mm3(bank[:, m * S:(m + 1) * S], act_hi[:, k, m * P:(m + 1) * P],
                                  act_lo[:, k, m * P:(m + 1) * P], wh[:, c], wl[:, c],
                                  start=first and c == 0 and m == 0)
                ins.then_inc(mm_done, 1)

            for kt in range(4):
                pe.wait_ge(xlo, 4 * kt + 4)
                pe.wait_ge(lo_done, kt + 1)
                wh, wl = with_gates(hi, kt), with_gates(lo, kt)
                for c in range(4):
                    for m, bank in enumerate((acc[0], acc[2])):
                        k = 4 * kt + c
                        ins = mm3(bank[:, 0:VA_COLS], act_hi[:, k, m * P:(m + 1) * P],
                                  act_lo[:, k, m * P:(m + 1) * P], wh[:, c], wl[:, c], start=k == 0)
                    if kt < 2 and c == 1:
                        turn_x_pair(2 * kt + 4)
                        turn_x_pair(2 * kt + 5)
                ins.then_inc(mm_done, 1)
            for kt in range(4):
                features(T_KA + kt, kt, acc[1], kt, act_hi, act_lo, kt == 0)
                if kt == 2:
                    pe.wait_ge(ones_s, 1)
                    pe.wait_ge(diag_done, 2)
                    for m in range(MT):
                        ins = pe.matmul(sc_ps[:, 0, m * P:(m + 1) * P], ones[:], diag[:, m], start=True, stop=True)
                    ins.then_inc(rms1_ps, 1)
                if kt == 3:
                    pe.wait_ge(nlf_s, 2)
                    pe.wait_ge(tri_s, 1)
                    for m in range(MT):
                        for k in range(m + 1):
                            t0 = 0 if k == m else P
                            for n, part in enumerate((nlf_hi, nlf_lo)):
                                ins = pe.matmul(pv_ps[:, m * NH:(m + 1) * NH], tri[:, t0:t0 + P], part[:, k],
                                                start=m == 0 and k == 0 and n == 0, stop=True, skip_group_check=True)
                    ins.then_inc(fcum_ps, 1)
                if kt == 3:
                    pe.wait_ge(d_cnv, 64)
                    pe.wait_ge(fcum_s, 1)
                    for j in range(4):
                        ins = pe.transpose(pv_ps[:, 128 + 88 * j:216 + 88 * j], rows[0:88, 1 + j, :], ident[0:88, 0:88])
                    ins.then_inc(cst_t, 1)

            def attention(s, slots, q):
                for e in slots.get(s, []):
                    p = int(e[1])
                    if e[0] == "S":
                        if p == 0:
                            pe.wait_ge(quad_s, q + 1)
                            pe.wait_ge(evac_a, q + 2)
                            pe.wait_ge(evac_d, q * 3 + 4)
                        pe.wait_ge(read_s, q * 4 + (p + 1))
                        for c0, c1, qs, n in ((0, 128, 0, 128), (128, 384, 128, 256)):
                            for h in range(2):
                                half = slice(h * HD, (h + 1) * HD)
                                qv, kv = (qa[half, p], kq[half]) if p < 2 else (qf[half, p - 2], kf[half, p - 2])
                                ins = pe.matmul(sc_ps[:, h, c0:c1], qv[:, qs:qs + 128], kv[:, 0:n], start=c0 == 0,
                                                stop=p < 2, skip_group_check=True)
                        if p >= 2:
                            for h in range(2):
                                i = (p - 2) * 2 + h
                                for n in range(2):
                                    for k, c0, c1, t0 in ((0, 0, 128, 0), (0, 128, 384, 0), (1, 256, 384, 0)):
                                        ins = pe.matmul(sc_ps[:, h, c0:c1], nlfq[:, n, k, i:i + 1].broadcast_to([P, P]),
                                                        tri[:, t0:t0 + c1 - c0], start=False, stop=True,
                                                        skip_group_check=True)
                        ins.then_inc(scores_s, 1)
                    if e[0] == "T":
                        pe.wait_ge(prob_s, q * 4 + (p + 1))
                        for h in range(2):
                            for c in range(3):
                                ins = pe.transpose(tr_ps[:, h, c * P:(c + 1) * P], prob[:, p, h, c * P:(c + 1) * P], ident[:])
                        ins.then_inc(pt_ps, 1)
                    if e[0] == "V":
                        pe.wait_ge(pt_s, q * 4 + (p + 1))
                        pe.wait_ge(mixlo_s, q * 4 + (p + 1))
                        for h in range(2):
                            i = (p - 2) * 2 + h
                            v = vq[:] if p < 2 else vf[:, :, i * HD:(i + 1) * HD]
                            half = slice(h * HD, (h + 1) * HD)
                            pe.matmul(pv_ps[half, 0:S], v[:, 0], prob_t[:, p % 2, h, 0:S], start=True, stop=False,
                                      skip_group_check=True)
                            ins = pe.matmul(pv_ps[half, P:S], v[:, 1], prob_t[:, p % 2, h, S:384], start=False, stop=True,
                                            skip_group_check=True)
                        ins.then_inc(pv_s, 1)

            def quad(j, attend):
                for s in range(QUAD_TILES):
                    n, kt = divmod(s, 4)
                    if kt == 0:
                        if n == 0:
                            if attend:
                                pe.wait_ge(evac_d, j * 3 + 1)
                            else:
                                pe.wait_ge(evac_a, 1)
                        if n == 1:
                            if attend:
                                pe.wait_ge(evac_a, j + 1)
                            else:
                                pe.wait_ge(swap_s, 1)
                                pe.wait_ge(evac_d, 1)
                        if n == 2:
                            pe.wait_ge(swap_s, j + 2)
                            pe.wait_ge(evac_d, j * 3 + 2)
                        if n == 3:
                            pe.wait_ge(evac_d, j * 3 + 3)
                    t = j * QUAD_TILES + (T_QUAD + s)
                    if n < 3:
                        features(t, kt, acc[n % 2], kt, act_hi, act_lo, kt == 0)
                    else:
                        tokens(t, kt, acc[1], kt, kt == 0)
                    if attend:
                        attention(s, SLOTS_LOOP, j - 1)

            quad(0, False)
            with pe.Fori(1, QUADS) as j:
                quad(j, True)

            def turn_x(u):
                pe.wait_ge(xcols_s, u + 1)
                for b in range(2):
                    for m in range(MT):
                        ins = pe.transpose(sc_ps[:, 0, b * S + m * P:b * S + (m + 1) * P],
                                           xcols[:, m, b * P:(b + 1) * P], ident[:])
                ins.then_inc(xt_ps, 1)

            def turn_y(u, par):
                pe.wait_ge(yt_s, u + 1)
                if not (isinstance(u, int) and u == 0):
                    pe.wait_ge(ynat_s, u)
                for m in range(MT):
                    for b in range(2):
                        ins = pe.transpose(sc_ps[:, 1, m * S + b * P:m * S + (b + 1) * P],
                                           yt[:, par, b, m * P:(m + 1) * P], ident[:])
                ins.then_inc(yt_ps, 1)

            for s, (u, kt) in enumerate(WOA_ORDER):
                if s == 0:
                    pe.wait_ge(evac_d, 3 * QUADS + 1)
                if s == 1:
                    pe.wait_ge(evac_a, QUADS + 1)
                if s == 6:
                    pe.wait_ge(mixlo_s, 4 * (QUADS - 1) + 3)
                if s == 9:
                    pe.wait_ge(mixlo_s, 4 * QUADS + 1)
                features(T_WOA + s, s % RING, acc[u], kt, mix_hi, mix_lo, kt == 0)
                attention(s, SLOTS_TAIL, QUADS - 1)
                if 8 <= s < 11:
                    if s == 8:
                        pe.wait_ge(read_s, 4 * QUADS + 1)
                    else:
                        pe.wait_ge(xts_s, s - 8)
                    turn_x(s - 8)
                if s >= 10:
                    turn_y(s - 10, s % 2)

            def wo_unit(u, par, bank, free):
                pe.wait_ge(yt_s, free)
                for s in range(4):
                    features(u * 4 + (T_WOB - 4 * WOA_UNITS + s), s, bank, s, mix_hi, mix_lo, s == 0)
                    if s == 0:
                        turn_y(u - 1, 1 - par)
                    if s == 2:
                        pe.wait_ge(xts_s, u)
                        turn_x(u)

            wo_unit(WOA_UNITS, WOA_UNITS % 2, acc[0], 1)
            with pe.Fori(0, 2) as i:
                wo_unit(i * 2 + 4, 0, acc[1], i * 2 + 3)
                wo_unit(i * 2 + 5, 1, acc[0], i * 2 + 4)

            def up_step(i, first):
                for s in range(UP_TILES):
                    v, kt = divmod(s, 4)
                    if kt == 0:
                        if first:
                            pe.wait_ge(yt_s, WO_UNITS - 1)
                        else:
                            pe.wait_ge(u_s, i * 4 + (2 * v - 2))
                    if first and v == 0:
                        pe.wait_ge(ylo_s, 2 * kt + 2)
                    features(i * UP_TILES + (T_UP + s), kt, acc[2 - v], kt, act_hi, act_lo, kt == 0)
                    if first and s == 0:
                        turn_y(WO_UNITS - 1, 1)
                        pe.wait_ge(ysum_s, WO_UNITS)
                        for b in range(2):
                            ins = pe.matmul(pv_ps[:, 0:S], ones[:], ysum[:, b], start=b == 0, stop=b == 1)
                        ins.then_inc(y2_ps, 1)

            up_step(0, True)
            with pe.Fori(1, UP_STEPS) as i:
                up_step(i, False)

            pe.wait_ge(ynat_s, WO_UNITS)
            with pe.Fori(0, GROUPS // 2) as g:
                for k in range(2 * DOWN_TILES):
                    n, kt = divmod(k, DOWN_TILES)
                    bank = sc_ps if n == 0 else tr_ps
                    pe.wait_ge(glo_s, kt + 1)
                    if kt == 0:
                        pe.wait_ge(z_s, g * 4 + (2 * n + 2))
                    pe.wait_ge(lo_done, g * (2 * DOWN_TILES) + (T_DOWN + k + 1))
                    wh, wl = wide(hi, k % RING), wide(lo, k % RING)
                    for c in range(2):
                        for m in range(MT):
                            b = 2 * kt + c
                            ins = mm3(bank[:, m], g_hi[:, b, m * P:(m + 1) * P], g_lo[:, b, m * P:(m + 1) * P],
                                      wh[:, c], wl[:, c], start=kt == 0 and c == 0)
                    ins.then_inc(mm_done, 1)


def constants():
    pos = np.arange(S)
    inv = (1.0 / (np.float32(10000.0) ** (np.arange(HD // 2, dtype=np.float32) * np.float32(2.0 / HD)))).astype(np.float32)
    ang = (pos.astype(np.float32)[None, :] * inv[:, None]).astype(np.float32)
    cos, sin = np.cos(ang).astype(np.float32), np.sin(ang).astype(np.float32)
    tri = np.triu(np.ones((P, P), np.float32))
    q, k = np.arange(P)[:, None], np.arange(S)[None, :]

    def mask(valid):
        both = np.concatenate([valid(q, k[:, :P]), valid(q + P, k)], axis=1)
        return np.where(both, 0.0, -1e30).astype(np.float32)

    return {
        "ident_c": np.eye(P, dtype=np.float32),
        "tri_c": np.concatenate([tri, np.ones((P, P), np.float32)], axis=1),
        "mask_a_c": mask(lambda q, k: (q // 64 - k // 64 >= 0) & (q // 64 - k // 64 <= 1)),
        "mask_b_c": mask(lambda q, k: k <= q),
        "cos_c": np.concatenate([cos] * 4),
        "sin_c": np.concatenate([-sin, sin] * 2),
    }


NAMES = ("x", "norm_mix", "w_in", "sinks", "b_f", "w_o", "norm_ffn", "w_up", "conv_w", "conv_b", "w_down", "norm_final")


def kernel(**inputs):
    import concourse.bacc as bacc
    from concourse.bass_utils import run_bass_kernel_spmd

    nc = bacc.Bacc("TRN2", target_bir_lowering=False, num_devices=1)
    arrays = {name: np.ascontiguousarray(inputs[name]) for name in NAMES}
    arrays.update(constants())
    args = [nc.dram_tensor(name, a.shape, mybir.dt.from_np(a.dtype), kind="ExternalInput").ap()
            for name, a in arrays.items()]
    result = nc.dram_tensor("result", (1, S, D), F32, kind="ExternalOutput").ap()
    program(nc, *args, result)
    return run_bass_kernel_spmd(nc, [arrays], core_ids=[0]).results[0]["result"]
```

```python
import numpy as np
import concourse.bass as bass
from concourse import mybir
from contextlib import ExitStack

F32 = mybir.dt.float32
R32 = mybir.dt.float32r
ALU = mybir.AluOpType
ACT = mybir.ActivationFunctionType
AX = mybir.AxisListType

P = 128
D = 2048
S = 256
KB = D // P
MT = S // P
HD = 64
NKV = 4
NH = 16
F = 5632
FB = F // P
EPS = 1e-5
QSCALE = HD ** -0.5
COL_QA, COL_KA, COL_VA = 0, 1024, 1280
COL_QF, COL_KF, COL_VF, COL_F = 1536, 2560, 3584, 4608

RING = 4
WARM = 9
WARM_AGAIN = 13
LEAD = 3
TILE = 1024
VA_COLS = 256 + NH
SLOT = 4 * VA_COLS
QUADS = 4
UP_STEPS = FB // 2
QUAD_STEPS = 13
UP_DVE_STEPS = 4
GROUPS = D // 512
DOWN_TILES = FB // 2

T_KA = 4
T_QUAD = 8
QUAD_TILES = 16
T_WOA = T_QUAD + QUADS * QUAD_TILES
WOA_UNITS = 3
T_WOB = T_WOA + 4 * WOA_UNITS
WO_UNITS = 8
T_UP = T_WOB + 4 * (WO_UNITS - WOA_UNITS)
UP_TILES = 8
T_DOWN = T_UP + UP_STEPS * UP_TILES
OUT_CUTS = (0, 512, 1536, D)
LAST = RING
T_END = T_DOWN + GROUPS * DOWN_TILES
WOA_ORDER = [(u, kt) for kt in (0, 2, 1, 3) for u in range(WOA_UNITS)]

SLOTS_LOOP = {0: ["S0"], 2: ["S1"], 3: ["T0"], 4: ["V0", "S2"], 5: ["T1"], 6: ["V1", "S3"], 7: ["T2"],
              8: ["V2"], 9: ["T3"], 10: ["V3"]}
SLOTS_TAIL = {0: ["S0"], 1: ["S1"], 2: ["S2"], 3: ["T0", "S3"], 4: ["V0", "T1"], 5: ["V1", "T2"],
              6: ["V2", "T3"], 7: ["V3"]}


X_THEN = [3, 7, 11]
BIAS_SLOTS = [7, 10, 11, 13]


def at_slot(slots, s, kind):
    return [int(e[1]) for e in slots.get(s, []) if e[0] == kind]


class Steps:

    def __init__(self, eng, sem):
        self.eng, self.sem, self.base, self.k, self.i, self.per = eng, sem, 0, 0, 0, 0

    def loop(self, i, first, per):
        self.base, self.k = self.base + self.k - first * per, 0
        self.i, self.per = i, per

    def end(self, passes_end):
        assert self.k == self.per, f"steps per pass: {self.k}"
        self.base, self.k, self.i, self.per = self.base + passes_end * self.per, 0, 0, 0

    def done(self, ins):
        ins.then_inc(self.sem, 1)
        self.k += 1

    def wait(self):
        self.eng.wait_ge(self.sem, self.i * self.per + (self.base + self.k))


class Sbuf:

    def __init__(self, nc):
        self.nc, self.cursor = nc, (nc.sbuf_base + 63) // 64 * 64

    def place(self, name, shape, dt=F32):
        t = self.nc.alloc_sbuf_tensor_at(name, shape, dt, offset=self.cursor)
        self.cursor += (4 * int(np.prod(shape[1:])) + 31) // 32 * 32
        return t


def program(nc, x, norm_mix, w_in, sinks, b_f, w_o, norm_ffn, w_up, conv_w, conv_b, w_down, norm_final,
            ident_c, tri_c, mask_a_c, mask_b_c, cos_c, sin_c, out):
    ctx = ExitStack()
    with ctx:
        sbuf = Sbuf(nc)
        sb = sbuf.place

        def ps(name, shape):
            return ctx.enter_context(nc.psum_tensor(name, shape, F32))

        def sem(name):
            return ctx.enter_context(nc.semaphore(name))

        raw = sb("raw", [P, RING, SLOT])
        hi = sb("hi", [P, RING, SLOT], R32)
        lo = sb("lo", [P, RING, SLOT], R32)
        nat = sb("nat", [P, MT, D])
        act_hi = sb("act_hi", [P, KB, S], R32)
        act_lo_at = sbuf.cursor
        act_lo = sb("act_lo", [P, KB, S], R32)
        ident = sb("ident", [P, P])
        ones = sb("ones", [P, P])
        cst = sb("cst", [P, 384])
        r2b = sb("r2b", [P, S])
        small = sb("small", [P, 96])

        region = sbuf.cursor
        g_hi = sb("g_hi", [P, FB, S], R32)
        g_lo = sb("g_lo", [P, FB, S], R32)
        region_end = sbuf.cursor
        sbuf.cursor = region
        mix_hi = sb("mix_hi", [P, KB, S], R32)
        mix_lo = sb("mix_lo", [P, KB, S], R32)
        va = sb("va", [P, MT, S])
        kta = sb("kta", [P, NKV, S])
        kq = sb("kq", [P, S])
        vq = sb("vq", [P, MT, HD])
        qa = sb("qa", [P, 2, S])
        kf = sb("kf", [P, 2, S])
        qf = sb("qf", [P, 2, S])
        vf = sb("vf", [P, MT, S])
        prob = sb("prob", [P, 4, 2, 384])
        prob_t = sb("prob_t", [P, 2, 2, 384])
        cos_r = sb("cos_r", [P, S])
        sin_r = sb("sin_r", [P, S])
        swap = sb("swap", [P, 2, S])
        rope_a = sb("rope_a", [P, 2, S])
        r1b = sb("r1b", [P, S])
        mask_a = sb("mask_a", [P, 384])
        mask_b = sb("mask_b", [P, P])
        fg = sb("fg", [P, 8, MT, NH])
        nlf_hi = sb("nlf_hi", [P, MT, NH], R32)
        nlf_lo = sb("nlf_lo", [P, MT, NH], R32)
        nft = sb("nft", [NH, S])
        fcum = sb("fcum", [P, MT, NH])
        fq = sb("fq", [P, MT, 4])
        nsink = sb("nsink", [P, MT, NH])
        nsq = sb("nsq", [P, MT, 4])
        stat = sb("stat", [P, 4, 5, 4])
        bf_b = sb("bf_b", [P, NH])
        key_bias_at = sbuf.cursor
        cos_t = sb("cos_t", [P, S])
        sin_t = sb("sin_t", [P, S])
        rope_b = sb("rope_b", [P, 2, S])
        diag = sb("diag", [P, MT, P])
        tri_f = sb("tri_f", [P, S])
        tri = sb("tri", [P, S], R32)
        sbuf.cursor = key_bias_at
        key_bias = sb("key_bias", [P, NH, 384])

        assert key_bias_at <= region_end and sbuf.cursor <= nc.sbuf_usable_end
        sbuf.cursor = region_end
        ub = sb("ub", [P, 2, 2, S + 2])
        conv_o = sb("conv_o", [P, 2, 2, S])
        silu = sb("silu", [P, 2, S])
        top = sbuf.cursor
        sbuf.cursor = region_end
        xts = sb("xts", [P, 2, S])
        yt = sb("yt", [P, 2, 2, S])
        ysq = sb("ysq", [P, 2, S])
        ysum = sb("ysum", [P, 2, S])
        xcols = sb("xcols", [P, MT, 2 * P])
        assert max(top, sbuf.cursor) <= nc.sbuf_usable_end
        sbuf.cursor = act_lo_at
        gfin = sb("gfin", [P, D])
        sq_out = sb("sq_out", [P, MT, 512])

        acc = [ps(f"acc{i}", [P, 512]) for i in range(3)]
        sc_ps = ps("sc_ps", [P, 2, 512])
        tr_ps = ps("tr_ps", [P, 2, 512])
        pv_ps = ps("pv_ps", [P, 512])
        x_banks = [acc[0][:], acc[2][:], acc[1][:], sc_ps[:, 0], sc_ps[:, 1], tr_ps[:, 0], tr_ps[:, 1], pv_ps[:]]

        d_w = [sem(f"d_w{i}") for i in range(RING)]
        d_x = [sem(f"d_x{i}") for i in range(4)]
        d_bias = [sem(f"d_bias{i}") for i in range(4)]
        d_id, d_nrm, d_cnv, d_cst, d_gf, d_out = (sem(n) for n in (
            "d_id", "d_nrm", "d_cnv", "d_cst", "d_gf", "d_out"))
        hi_done, lo_done, mm_done = sem("hi_done"), sem("lo_done"), sem("mm_done")
        act_step, dve_step, pool_step = sem("act_step"), sem("dve_step"), sem("pool_step")
        cst_t, cst_c = sem("cst_t"), sem("cst_c")
        x_t, xhi, xlo = sem("x_t"), sem("xhi"), sem("xlo")
        evac_d, evac_a = sem("evac_d"), sem("evac_a")
        ones_s = sem("ones_s")
        rms1_root, rms1_done, diag_done, rms1_ps, r1b_done = (sem(n) for n in (
            "rms1_root", "rms1_done", "diag_done", "rms1_ps", "r1b_done"))
        f_abs, f_ln, nlf_s, fcum_ps, fcum_s, nft_ps, nft_s, nft_out, bias_s = (sem(n) for n in (
            "f_abs", "f_ln", "nlf_s", "fcum_ps", "fcum_s", "nft_ps", "nft_s", "nft_out",
            "bias_s"))
        tri_s, kta_s, swap_s, krope_s, nsink_s, quad_s = (sem(n) for n in (
            "tri_s", "kta_s", "swap_s", "krope_s", "nsink_s", "quad_s"))
        scores_s, read_s, negmax_s, exp_s, prob_s, pt_ps, pt_s, pv_s, mixhi_s, mixlo_s = (sem(n) for n in (
            "scores_s", "read_s", "negmax_s", "exp_s", "prob_s", "pt_ps", "pt_s", "pv_s", "mixhi_s", "mixlo_s"))
        xcols_s, xt_ps, xts_s, yt_s, ysq_s, yhi_s, ylo_s, yt_ps, ynat_s, ysum_s, y2_ps, y2_root, r2_s = (sem(n) for n in (
            "xcols_s", "xt_ps", "xts_s", "yt_s", "ysq_s", "yhi_s", "ylo_s", "yt_ps", "ynat_s", "ysum_s", "y2_ps",
            "y2_root", "r2_s"))
        pad_s, u_s, c0_s, conv_s, silu_s, gated_s, ghi_s, glo_s = (sem(n) for n in (
            "pad_s", "u_s", "c0_s", "conv_s", "silu_s", "gated_s", "ghi_s", "glo_s"))
        z_s, zsq_s, z_tot, z_root, z_rms, fin_a, fin_d, part_s, last_s = (sem(n) for n in (
            "z_s", "zsq_s", "z_tot", "z_root", "z_rms", "fin_a", "fin_d", "part_s", "last_s"))

        nft_dram = nc.dram_tensor("nft_dram", (NH, S), F32).ap()

        win = w_in[0].rearrange("(t c p) n -> t p c n", p=P, c=4)
        wo = w_o[0].rearrange("(t c p) n -> t p c n", p=P, c=4)
        wup = w_up[0].rearrange("(t c p) n -> t p c n", p=P, c=4)
        wdn = w_down[0].rearrange("(t c p) n -> t p c n", p=P, c=2)

        def narrow(t, slot):
            return t[:, slot, 0:TILE].rearrange("p (c n) -> p c n", c=4)

        def wide(t, slot):
            return t[:, slot, 0:TILE].rearrange("p (c n) -> p c n", c=2)

        def with_gates(t, slot):
            return t[:, slot].rearrange("p (c n) -> p c n", c=4)

        flat = prob[:].rearrange("p a b n -> p (a b n)")
        rows = flat[:, D:D + 5 * P].rearrange("p (j n) -> p j n", j=5)
        eps = small[:, 0:1]
        ss1 = small[:, 2:4]
        root1 = small[:, 4:6]
        r1c = small[:, 6:8]
        ss3 = small[:, 8:16].rearrange("p (m g) -> p m g", m=2)
        part3 = small[:, 16:18]
        root3 = small[:, 18:20]
        r3 = small[:, 20:22]
        g1 = cst[:, 0:KB]
        g2 = cst[:, KB:2 * KB]

        def tap(j, b, n=1):
            return cst[:, bass.ds(32 + 88 * j + b, n)]

        block = ctx.enter_context(nc.Block())

        @block.sync
        def _(sp):
            sp.dma_start(rows[0:KB, 0], norm_mix.rearrange("a (b p) -> (a b) p", p=P)).then_inc(d_nrm, 16)
            def load_x(c):
                for m in range(MT):
                    sp.dma_start(nat[:, m, c * 512:(c + 1) * 512],
                                 x[0, m * P:(m + 1) * P, c * 512:(c + 1) * 512]).then_inc(d_x[c], 16)

            load_x(0)
            for c in range(4):
                if c == 0:
                    load_x(1)
                elif c < 3:
                    load_x(c + 1)
                sp.dma_start(with_gates(raw, c)[:, :, 0:256], win[c][:, :, COL_VA:COL_VA + 256]).then_inc(d_w[c], 16)
                sp.dma_start(with_gates(raw, c)[:, :, 256:VA_COLS], win[c][:, :, COL_F:COL_F + NH]).then_inc(d_w[c], 16)

            def load(t, slot, dst, src):
                sp.wait_ge(lo_done, t - (RING - 1))
                sp.dma_start(dst, src).then_inc(d_w[slot], 16)

            def load_unit(t, w, col, kts=range(4)):
                for k, kt in enumerate(kts):
                    load(t + k, k, narrow(raw, k), w[kt][:, :, bass.ds(col, 256)])

            load_unit(T_KA, win, COL_KA)
            with sp.Fori(0, QUADS) as j:
                for n, col in enumerate((COL_QA, COL_KF, COL_QF, COL_VF)):
                    load_unit(j * QUAD_TILES + (T_QUAD + 4 * n), win, j * 256 + col)
            for n, (u, kt) in enumerate(WOA_ORDER):
                load(T_WOA + n, n % RING, narrow(raw, n % RING), wo[kt][:, :, u * 256:(u + 1) * 256])
            with sp.Fori(0, WO_UNITS - WOA_UNITS) as u:
                load_unit(u * 4 + T_WOB, wo, u * 256 + WOA_UNITS * 256)
            with sp.Fori(0, UP_STEPS) as i:
                load_unit(i * UP_TILES + T_UP, wup, i * 256)
                load_unit(i * UP_TILES + (T_UP + 4), wup, i * 256 + F)
            with sp.Fori(0, GROUPS // 2) as g:
                for k in range(2 * DOWN_TILES):
                    n, kt = divmod(k, DOWN_TILES)
                    load(g * (2 * DOWN_TILES) + (T_DOWN + k), k % RING, wide(raw, k % RING),
                         wdn[kt][:, :, bass.ds(g * 1024 + n * 512, 512)])
            sp.wait_ge(fin_d, 1)
            sp.dma_start(out[0, 0:P, OUT_CUTS[1]:OUT_CUTS[2]], nat[:, 0, OUT_CUTS[1]:OUT_CUTS[2]]).then_inc(d_out, 16)
            sp.wait_ge(fin_a, 1)
            sp.dma_start(out[0, 0:P, 0:OUT_CUTS[1]], nat[:, 0, 0:OUT_CUTS[1]]).then_inc(d_out, 16)
            sp.wait_ge(fin_d, 2)
            sp.dma_start(out[0, 0:P, OUT_CUTS[2]:D], nat[:, 0, OUT_CUTS[2]:D]).then_inc(d_out, 16)
            sp.wait_ge(fin_d, 3)
            sp.dma_start(out[0, P:2 * P, OUT_CUTS[1]:OUT_CUTS[2]], nat[:, 1, OUT_CUTS[1]:OUT_CUTS[2]]).then_inc(d_out, 16)
            sp.wait_ge(fin_d, 4)
            sp.dma_start(out[0, P:2 * P, OUT_CUTS[2]:D], nat[:, 1, OUT_CUTS[2]:D]).then_inc(d_out, 16)
            sp.wait_ge(d_out, 96)

        @block.gpsimd
        def _(pool):
            pool.memset(ones[:], 1.0).then_inc(ones_s, 1)
            for j in range(3):
                pool.dma_start(rows[0:2 * FB, 1 + j], conv_w[0, j].rearrange("(b p) -> b p", p=P)).then_inc(d_cnv, 16)
            pool.dma_start(rows[0:2 * FB, 4], conv_b.rearrange("a (b p) -> (a b) p", p=P)).then_inc(d_cnv, 16)
            for dst, src in ((cos_t[:], cos_c), (sin_t[:], sin_c), (tri_f[:], tri_c), (mask_a[:], mask_a_c),
                             (mask_b[:], mask_b_c), (nsink[:, 0], sinks[0].partition_broadcast(P)),
                             (nsink[:, 1], sinks[0].partition_broadcast(P)), (bf_b[:], b_f[0].partition_broadcast(P))):
                pool.dma_start(dst, src).then_inc(d_cst, 16)
            for c in range(4):
                pool.wait_ge(d_x[c], 32)
            pool.wait_ge(kta_s, 4)
            pool.wait_ge(evac_a, 1)
            pool.wait_ge(nlf_s, 2)
            pool.wait_ge(fcum_s, 1)
            pool.wait_ge(nsink_s, 1)
            pool.wait_ge(nft_s, 1)
            pool.dma_start(nft_dram, nft[:]).then_inc(nft_out, 16)
            pool.wait_ge(nft_out, 16)
            for n in range(4):
                pool.dma_start(key_bias[:, 4 * n:4 * n + 4, P:384],
                               nft_dram[4 * n:4 * n + 4].partition_broadcast(P)).then_inc(d_bias[n], 16)
            with pool.Fori(0, QUADS) as j:
                pool.wait_ge(mixlo_s, j * 4 + 1)
                pool.tensor_copy(kq[:], kta[:, bass.ds(j, 1), :].rearrange("p a n -> p (a n)"))
                pool.tensor_copy(vq[:], va[:, :, bass.ds(j * HD, HD)])
                pool.tensor_copy(fq[:], fcum[:, :, bass.ds(j * 4, 4)])
                pool.tensor_copy(nsq[:], nsink[:, :, bass.ds(j * 4, 4)]).then_inc(quad_s, 1)
            pool.wait_ge(read_s, 4 * QUADS + 1)
            pool.tensor_copy(xcols[:], nat[:, :, 0:2 * P]).then_inc(xcols_s, 1)
            with pool.Fori(1, WO_UNITS) as u:
                pool.wait_ge(xt_ps, u)
                pool.tensor_copy(xcols[:], nat[:, :, bass.ds(u * 2 * P, 2 * P)]).then_inc(xcols_s, 1)
            pool.wait_ge(mm_done, T_DOWN)
            pool.dma_start(gfin[:], norm_final.partition_broadcast(P)).then_inc(d_gf, 16)

        @block.scalar
        def _(act):
            act.dma_start(ident[:], ident_c).then_inc(d_id, 16)
            act.dma_start(rows[KB:2 * KB, 0], norm_ffn.rearrange("a (b p) -> (a b) p", p=P)).then_inc(d_nrm, 16)
            st = Steps(act, act_step)

            def split_hi(t, slot):
                act.wait_ge(d_w[slot], (t - slot) * (16 // RING) + 32)
                if not (isinstance(t, int) and t < RING):
                    act.wait_ge(mm_done, t - (RING - 1))
                n = SLOT if isinstance(t, int) and t < T_KA else TILE
                act.activation(hi[:, slot, 0:n], raw[:, slot, 0:n], ACT.Copy).then_inc(hi_done, 1)

            act.wait_ge(cst_t, 1)
            act.activation(cst[:, 0:2 * KB], pv_ps[:, 0:2 * KB], ACT.Copy).then_inc(cst_c, 1)
            act.wait_ge(cst_c, 1)
            for c in range(KB):
                act.wait_ge(x_t, c // 2 + 1)
                act.activation(act_hi[:, c], x_banks[c // 2][:, (c % 2) * S:(c % 2 + 1) * S], ACT.Copy,
                               scale=g1[:, c:c + 1]).then_inc(xhi, 1)
                if c in X_THEN:
                    split_hi(X_THEN.index(c), X_THEN.index(c))

            def rope_swap(bank, scale):
                for o in range(0, P, 32):
                    i = o ^ 32
                    ins = act.activation(swap[o:o + 32].rearrange("p a n -> p (a n)"), bank[i:i + 32, :], ACT.Copy, scale=scale)
                ins.then_inc(swap_s, 1)

            def values(bank, dst):
                act.activation(dst[:, 0], bank[:, 0:S], ACT.Copy, scale=r1c[:, 0:1])
                act.activation(dst[:, 1], bank[:, S:2 * S], ACT.Copy, scale=r1c[:, 1:2]).then_inc(evac_a, 1)

            split_hi(3, 3)
            act.wait_ge(d_x[3], 32)
            for m in range(MT):
                split_hi(4 + m, m)
                if m > 0:
                    st.wait()
                st.done(act.activation(flat[:, 0:D], nat[:, m, :], ACT.Square, accum_out=ss1[:, m:m + 1]))
            act.wait_ge(pad_s, 1)
            st.wait()
            act.activation(root1, ss1, ACT.Sqrt, bias=eps, scale=1.0 / D).then_inc(rms1_root, 1)
            split_hi(6, 2)
            for s in range(4):
                split_hi(T_KA + s + LEAD, (s + LEAD) % RING)
                if s == 0:
                    act.wait_ge(rms1_done, 1)
                    act.wait_ge(mm_done, 4)
                    for m, bank in enumerate((acc[0], acc[2])):
                        ins = act.activation(va[:, m], bank[:, 0:256], ACT.Copy, scale=r1c[:, m:m + 1])
                    ins.then_inc(evac_a, 1)
                if s == 1:
                    act.wait_ge(f_abs, 1)
                    st.done(act.activation(fg[:, 2], fg[:, 1], ACT.Exp, scale=-1.0))
                    st.wait()
                    act.activation(fg[:, 3], fg[:, 2], ACT.Ln, bias=1.0).then_inc(f_ln, 1)
                if s == 2:
                    act.wait_ge(rms1_ps, 1)
                    act.activation(r1b[:], sc_ps[:, 0, 0:S], ACT.Copy).then_inc(r1b_done, 1)
                if s == 3:
                    act.wait_ge(mm_done, T_KA + 4)
                    rope_swap(acc[1], 1.0)
                    act.wait_ge(fcum_ps, 1)
                    act.activation(fcum[:].rearrange("p a n -> p (a n)"), pv_ps[:, 0:MT * NH], ACT.Copy,
                                   scale=-1.0).then_inc(fcum_s, 1)
                    act.wait_ge(krope_s, 1)
                    for h in range(2):
                        for e in range(2):
                            act.activation(kta[h * 64:h * 64 + 64, e::2, :], rope_b[e * 64:e * 64 + 64],
                                           ACT.Copy).then_inc(kta_s, 1)

            def attention(s, slots, q):
                for p in at_slot(slots, s - 1, "S"):
                    act.wait_ge(negmax_s, q * 4 + (p + 1))
                    for t in range(2):
                        for h in range(2):
                            pr = prob[:, p, h, 0:128] if t == 0 else prob[:, p, h, 128:384]
                            ins = act.activation(pr, pr, ACT.Exp, bias=stat[:, p, 0, 2 * t + h:2 * t + h + 1],
                                                 accum_out=stat[:, p, 1, 2 * t + h:2 * t + h + 1])
                    if p < 2:
                        ins = act.activation(stat[:, p, 3], stat[:, p, 2], ACT.Exp)
                    ins.then_inc(exp_s, 1)
                for e in slots.get(s, []):
                    p = int(e[1])
                    if e[0] == "T":
                        act.wait_ge(pt_ps, q * 4 + (p + 1))
                        act.activation(prob_t[:, p % 2], tr_ps[:, :, 0:384], ACT.Copy).then_inc(pt_s, 1)
                    if e[0] == "V":
                        act.wait_ge(pv_s, q * 4 + (p + 1))
                        chunk = q * 2 + (p if p < 2 else 8 + p - 2)
                        act.activation(mix_hi[:, bass.ds(chunk, 1), :].rearrange("p a n -> p (a n)"), pv_ps[:, 0:S],
                                       ACT.Copy).then_inc(mixhi_s, 1)

            def quad(j, attend):
                for s in range(QUAD_TILES):
                    split_hi(j * QUAD_TILES + (T_QUAD + s + LEAD), (s + LEAD) % RING)
                    if s == 4:
                        act.wait_ge(mm_done, j * QUAD_TILES + (T_QUAD + 4))
                        act.wait_ge(krope_s, j + 1)
                        rope_swap(acc[0], QSCALE)
                    if s == 15:
                        act.wait_ge(mm_done, j * QUAD_TILES + (T_QUAD + 16))
                        values(acc[1], vf)
                    if attend:
                        attention(s, SLOTS_LOOP, j - 1)
                    elif s == 1:
                        act.wait_ge(nft_ps, 1)
                        act.activation(nft[:], sc_ps[0:NH, 1, 0:S], ACT.Copy).then_inc(nft_s, 1)
                        act.wait_ge(cst_t, 2)
                        act.activation(cst[:, 2 * KB:384], pv_ps[:, 128:480], ACT.Copy).then_inc(cst_c, 1)

            quad(0, False)
            with act.Fori(1, QUADS) as j:
                quad(j, True)

            def take_xt(u):
                act.wait_ge(xt_ps, u + 1)
                if not (isinstance(u, int) and u == 0):
                    act.wait_ge(yt_s, u)
                act.activation(xts[:].rearrange("p a n -> p (a n)"), sc_ps[:, 0], ACT.Copy).then_inc(xts_s, 1)

            def after_y(u, par):
                act.wait_ge(yt_s, u + 1)
                if not (isinstance(u, int) and u == 0):
                    act.wait_ge(ysum_s, u)
                act.activation(ysq[:], yt[:, par], ACT.Square).then_inc(ysq_s, 1)
                for b in range(2):
                    act.activation(act_hi[:, bass.ds(u * 2 + b, 1), :].rearrange("p a n -> p (a n)"), yt[:, par, b],
                                   ACT.Copy, scale=cst[:, bass.ds(u * 2 + (KB + b), 1)]).then_inc(yhi_s, 1)

            def take_ynat(u):
                act.wait_ge(yt_ps, u + 1)
                act.activation(nat[:, :, bass.ds(u * 256, 256)], sc_ps[:, 1].rearrange("p (m n) -> p m n", m=2),
                               ACT.Copy).then_inc(ynat_s, 1)

            for s in range(4 * WOA_UNITS):
                split_hi(T_WOA + s + LEAD, (s + LEAD) % RING)
                attention(s, SLOTS_TAIL, QUADS - 1)
                if s >= 8 and s < 11:
                    take_xt(s - 8)
                if s >= 10:
                    take_ynat(s - 10)
                if s >= 9:
                    after_y(s - 9, (s - 9) % 2)

            def wo_unit(u, par):
                t = u * 4 + (T_WOB - 4 * WOA_UNITS)
                for s in range(4):
                    split_hi(t + (s + LEAD), (s + LEAD) % RING)
                    if s == 0:
                        take_ynat(u - 1)
                    if s == 2:
                        take_xt(u)
                    if s == 3:
                        after_y(u, par)

            wo_unit(WOA_UNITS, WOA_UNITS % 2)
            with act.Fori(0, 2) as i:
                wo_unit(i * 2 + 4, 0)
                wo_unit(i * 2 + 5, 1)

            def up_step(i, first):
                for s in range(UP_TILES):
                    split_hi(i * UP_TILES + (T_UP + s + LEAD), (s + LEAD) % RING)
                    if first and s == 0:
                        take_ynat(WO_UNITS - 1)
                    if first and s == 1:
                        act.wait_ge(y2_ps, 1)
                        act.activation(ysq[:, 0], pv_ps[:, 0:S], ACT.Sqrt, bias=eps, scale=1.0 / D).then_inc(y2_root, 1)
                    if s in (3, 7):
                        v = s // 4
                        for b in range(2):
                            act.wait_ge(u_s, i * 4 + (2 * v + b + 1))
                            act.activation(conv_o[:, v, b], ub[:, v, b, 2:S + 2], ACT.Identity,
                                           scale=tap(2, i * 2 + (b + v * FB)), bias=tap(3, i * 2 + (b + v * FB))).then_inc(c0_s, 1)
                    if s == 5:
                        act.wait_ge(conv_s, i * 4 + 2)
                        if not first:
                            act.wait_ge(glo_s, i)
                        act.activation(silu[:], conv_o[:, 0], ACT.Silu).then_inc(silu_s, 1)
                    if s == 7:
                        for b in range(2):
                            act.wait_ge(gated_s, i * 2 + (b + 1))
                            act.activation(g_hi[:, bass.ds(i * 2 + b, 1), :].rearrange("p a n -> p (a n)"), silu[:, b],
                                           ACT.Copy).then_inc(ghi_s, 1)

            up_step(0, True)
            with act.Fori(1, UP_STEPS) as i:
                up_step(i, False)

            def squares(n):
                if n > 0:
                    act.wait_ge(zsq_s, n)
                for m in range(MT):
                    act.wait_ge(z_s, 2 * n + (m + 5))
                    ins = act.activation(sq_out[:, m], nat[:, m, n * 512:(n + 1) * 512], ACT.Square,
                                         accum_out=ss3[:, m, n:n + 1])
                ins.then_inc(zsq_s, 1)

            act.activation(small[:, 24:25], eps, ACT.Sqrt)
            for t in range(GROUPS * DOWN_TILES):
                if T_DOWN + t + LEAD < T_END:
                    split_hi(T_DOWN + t + LEAD, (t + LEAD) % RING)
                if t % DOWN_TILES == DOWN_TILES - 1 and t < 3 * DOWN_TILES:
                    squares(t // DOWN_TILES)
            act.wait_ge(part_s, 1)
            for m in range(MT):
                act.wait_ge(z_s, 2 * 3 + m + 5)
                act.activation(sq_out[:, m], nat[:, m, 3 * 512:D], ACT.Square, accum_out=ss3[:, m, 3:4]).then_inc(zsq_s, 1)
                act.wait_ge(zsq_s, 4 + m)
                act.activation(root3[:, m:m + 1], ss3[:, m, 3:4], ACT.Sqrt, bias=part3[:, m:m + 1],
                               scale=1.0 / D).then_inc(z_root, 1)
                act.wait_ge(z_rms, m + 4)
                act.activation(nat[:, m, 0:OUT_CUTS[1]], nat[:, m, 0:OUT_CUTS[1]], ACT.Copy,
                               scale=r3[:, m:m + 1]).then_inc(fin_a, 1)
            act.wait_ge(fin_a, 2)
            act.dma_start(out[0, P:2 * P, 0:OUT_CUTS[1]], nat[:, 1, 0:OUT_CUTS[1]]).then_inc(d_out, 16)

        @block.vector
        def _(dve):
            st = Steps(dve, dve_step)

            def split_lo(t, slot):
                dve.wait_ge(hi_done, t + 1)
                n = SLOT if isinstance(t, int) and t < T_KA else TILE
                dve.tensor_tensor(lo[:, slot, 0:n], raw[:, slot, 0:n], hi[:, slot, 0:n].bitcast(F32),
                                  ALU.subtract).then_inc(lo_done, 1)

            dve.memset(small[:, 90:91], 0.0).then_inc(read_s, 1)
            dve.memset(small[:, 91:92], 0.0).then_inc(mixlo_s, 1)
            dve.memset(small[:, 92:93], 0.0).then_inc(z_s, 4)
            dve.memset(eps, EPS).then_inc(pad_s, 1)
            dve.wait_ge(cst_c, 1)
            for c in range(KB):
                dve.wait_ge(xhi, c // 2 * 2 + 2)
                dve.scalar_tensor_tensor(act_lo[:, c], x_banks[c // 2][:, (c % 2) * S:(c % 2 + 1) * S], g1[:, c:c + 1],
                                         act_hi[:, c].bitcast(F32), ALU.mult, ALU.subtract).then_inc(xlo, 1)
                if c in X_THEN:
                    split_lo(X_THEN.index(c), X_THEN.index(c))
            split_lo(3, 3)
            dve.wait_ge(d_cst, 128)
            dve.tensor_scalar(nsink[:], nsink[:], -1.0, None, ALU.mult).then_inc(nsink_s, 1)
            dve.tensor_copy(tri[:], tri_f[:]).then_inc(tri_s, 1)
            split_lo(4, 0)
            split_lo(5, 1)
            dve.wait_ge(rms1_root, 1)
            dve.reciprocal(r1c, root1).then_inc(rms1_done, 1)
            dve.wait_ge(rms1_done, 1)
            dve.wait_ge(d_id, 16)
            for m in range(MT):
                dve.tensor_scalar(diag[:, m], ident[:], r1c[:, m:m + 1], None, ALU.mult).then_inc(diag_done, 1)
            split_lo(6, 2)

            def rope(bank, scale, tmp):
                dve.scalar_tensor_tensor(tmp[:], bank[:].rearrange("p (a n) -> p a n", a=2), scale,
                                         cos_r[:].unsqueeze(1).broadcast_to([P, 2, S]), ALU.mult, ALU.mult).then_inc(evac_d, 1)

            def rope_rest(dst, tmp):
                st.done(dve.tensor_tensor(swap[:], swap[:], sin_r[:].unsqueeze(1).broadcast_to([P, 2, S]), ALU.mult))
                st.wait()
                return dve.tensor_tensor(dst[:], tmp[:], swap[:], ALU.add)

            for s in range(4):
                split_lo(T_KA + s + LEAD, (s + LEAD) % RING)
                if s == 1:
                    dve.wait_ge(evac_a, 1)
                    for m, bank in enumerate((acc[0], acc[2])):
                        st.done(dve.scalar_tensor_tensor(fg[:, 0, m], bank[:, 256:VA_COLS], r1c[:, m:m + 1],
                                                         bf_b[:], ALU.mult, ALU.add))
                    st.wait()
                    dve.scalar_tensor_tensor(fg[:, 1], fg[:, 0], -1.0, fg[:, 0], ALU.mult, ALU.max).then_inc(f_abs, 1)
                    st.done(dve.tensor_scalar(fg[:, 4], fg[:, 0], 0.0, None, ALU.min))
                    dve.wait_ge(f_ln, 1)
                    st.wait()
                    st.done(dve.tensor_tensor(fg[:, 5], fg[:, 3], fg[:, 4], ALU.subtract))
                    st.wait()
                    dve.tensor_copy(nlf_hi[:], fg[:, 5]).then_inc(nlf_s, 1)
                    dve.wait_ge(nlf_s, 1)
                    dve.tensor_tensor(nlf_lo[:], fg[:, 5], nlf_hi[:].bitcast(F32), ALU.subtract).then_inc(nlf_s, 1)
                if s == 2:
                    dve.wait_ge(r1b_done, 1)
                    st.done(dve.tensor_tensor(cos_r[:], cos_t[:], r1b[:], ALU.mult))
                    st.done(dve.tensor_tensor(sin_r[:], sin_t[:], r1b[:], ALU.mult))
                    st.wait()
                if s == 3:
                    dve.wait_ge(mm_done, T_KA + 4)
                    dve.wait_ge(swap_s, 1)
                    rope(acc[1], 1.0, rope_a)
                    dve.wait_ge(evac_d, 1)
                    rope_rest(rope_b, rope_a).then_inc(krope_s, 1)

            def attention(s, slots, q):
                for p in at_slot(slots, s - 1, "S"):
                    dve.wait_ge(exp_s, q * 4 + (p + 1))
                    if p < 2:
                        st.done(dve.tensor_tensor(stat[:, p, 1], stat[:, p, 1], stat[:, p, 3], ALU.add))
                        st.wait()
                    st.done(dve.reciprocal(stat[:, p, 4], stat[:, p, 1]))
                    st.wait()
                    for t in range(2):
                        for h in range(2):
                            pr = prob[:, p, h, 0:128] if t == 0 else prob[:, p, h, 128:384]
                            ins = dve.tensor_scalar(pr, pr, stat[:, p, 4, 2 * t + h:2 * t + h + 1], None, ALU.mult)
                    ins.then_inc(prob_s, 1)
                for e in slots.get(s, []):
                    p = int(e[1])
                    if e[0] == "S":
                        dve.wait_ge(scores_s, q * 4 + (p + 1))
                        if p < 2:
                            ins = dve.tensor_tensor(prob[:, p], sc_ps[:, :, 0:384],
                                                    mask_a[:].unsqueeze(1).broadcast_to([P, 2, 384]), ALU.add)
                        else:
                            dve.wait_ge(bias_s, 4)
                            bias = key_bias[:, bass.ds(q * 4, 4), :]
                            for t in range(2):
                                for h in range(2):
                                    c0, c1 = (0, 128) if t == 0 else (128, 384)
                                    i = (p - 2) * 2 + h
                                    ins = dve.scalar_tensor_tensor(prob[:, p, h, c0:c1], sc_ps[:, h, c0:c1],
                                                                   fq[:, t, i:i + 1], bias[:, i, c0:c1], ALU.add, ALU.add)
                        ins.then_inc(read_s, 1)
                        dve.wait_ge(read_s, q * 4 + (p + 2))
                        for t in range(2):
                            c0, c1 = (0, 128) if t == 0 else (128, 384)
                            ins = dve.tensor_reduce(stat[:, p, 0, 2 * t:2 * t + 2], prob[:, p, :, c0:c1], AX.X, ALU.max,
                                                    negate=True)
                            if p < 2:
                                st.done(ins)
                        if p < 2:
                            st.wait()
                            nsv = nsq[:, :, 2 * p:2 * p + 2]
                            mv = stat[:, p, 0].rearrange("p (t h) -> p t h", t=2)
                            st.done(dve.tensor_tensor(mv, mv, nsv, ALU.min))
                            st.wait()
                            ins = dve.tensor_tensor(stat[:, p, 2].rearrange("p (t h) -> p t h", t=2), mv, nsv, ALU.subtract)
                        ins.then_inc(negmax_s, 1)
                    if e[0] == "V":
                        dve.wait_ge(mixhi_s, q * 4 + (p + 1))
                        chunk = q * 2 + (p if p < 2 else 8 + p - 2)
                        mh = mix_hi[:, bass.ds(chunk, 1), :].rearrange("p a n -> p (a n)").bitcast(F32)
                        dve.tensor_tensor(mix_lo[:, bass.ds(chunk, 1), :].rearrange("p a n -> p (a n)"), pv_ps[:, 0:S], mh,
                                          ALU.subtract).then_inc(mixlo_s, 1)

            def quad(j, attend):
                for s in range(QUAD_TILES):
                    split_lo(j * QUAD_TILES + (T_QUAD + s + LEAD), (s + LEAD) % RING)
                    if s == 5:
                        dve.wait_ge(mm_done, j * QUAD_TILES + (T_QUAD + 4))
                        dve.wait_ge(swap_s, j + 2)
                        rope(acc[0], QSCALE, rope_a)
                    if s == 9:
                        dve.wait_ge(evac_d, j * 3 + 2)
                        rope_rest(qa, rope_a).then_inc(krope_s, 1)
                    if s in (8, 12):
                        dve.wait_ge(mm_done, j * QUAD_TILES + (T_QUAD + s))
                        bank, dst, scale = (acc[1], kf, 1.0) if s == 8 else (acc[0], qf, QSCALE)
                        dve.scalar_tensor_tensor(dst[:], bank[:].rearrange("p (a n) -> p a n", a=2), scale,
                                                 r1b[:].unsqueeze(1).broadcast_to([P, 2, S]), ALU.mult,
                                                 ALU.mult).then_inc(evac_d, 1)
                    if attend:
                        if s == 0:
                            dve.wait_ge(quad_s, j)
                        attention(s, SLOTS_LOOP, j - 1)
                    elif s in BIAS_SLOTS:
                        n = BIAS_SLOTS.index(s)
                        dve.wait_ge(d_bias[n], 16)
                        kb = key_bias[:, 4 * n:4 * n + 4, :]
                        mask = mask_b[:].unsqueeze(1).broadcast_to([P, 4, P])
                        dve.tensor_tensor(kb[:, :, 0:P], kb[:, :, P:2 * P], mask, ALU.add)
                        dve.tensor_tensor(kb[:, :, 2 * P:384], kb[:, :, 2 * P:384], mask, ALU.add).then_inc(bias_s, 1)

            quad(0, False)
            with dve.Fori(1, QUADS) as j:
                st.loop(j, 1, QUAD_STEPS)
                quad(j, True)
                st.end(QUADS)

            def make_y(u, par, bank):
                dve.wait_ge(xts_s, u + 1)
                if not (isinstance(u, int) and u < 2):
                    dve.wait_ge(yt_ps, u - 1)
                dve.tensor_tensor(yt[:, par].rearrange("p a n -> p (a n)"), bank[:], xts[:].rearrange("p a n -> p (a n)"),
                                  ALU.add).then_inc(yt_s, 1)
                dve.wait_ge(yt_s, u + 1)
                dve.wait_ge(ysq_s, u + 1)
                if not (isinstance(u, int) and u == 0):
                    dve.wait_ge(ysum_s, u)
                dve.tensor_tensor(ysum[:], ysum[:], ysq[:], ALU.add).then_inc(ysum_s, 1)
                for b in range(2):
                    dve.wait_ge(yhi_s, u * 2 + (b + 1))
                    ins = dve.scalar_tensor_tensor(
                        act_lo[:, bass.ds(u * 2 + b, 1), :].rearrange("p a n -> p (a n)"), yt[:, par, b],
                        cst[:, bass.ds(u * 2 + (KB + b), 1)],
                        act_hi[:, bass.ds(u * 2 + b, 1), :].rearrange("p a n -> p (a n)").bitcast(F32),
                        ALU.mult, ALU.subtract)
                ins.then_inc(ylo_s, 1)

            for s in range(4 * WOA_UNITS):
                split_lo(T_WOA + s + LEAD, (s + LEAD) % RING)
                if s == 0:
                    dve.wait_ge(quad_s, QUADS)
                attention(s, SLOTS_TAIL, QUADS - 1)
                if s >= 9:
                    dve.wait_ge(mm_done, T_WOA + s + 1)
                    if s == 9:
                        st.done(dve.memset(ysum[:], 0.0))
                        st.wait()
                    make_y(s - 9, (s - 9) % 2, acc[s - 9])

            def wo_unit(u, par, bank):
                t = u * 4 + (T_WOB - 4 * WOA_UNITS)
                for s in range(4):
                    split_lo(t + (s + LEAD), (s + LEAD) % RING)
                dve.wait_ge(mm_done, t + 4)
                make_y(u, par, bank)

            wo_unit(WOA_UNITS, WOA_UNITS % 2, acc[0])
            with dve.Fori(0, 2) as i:
                wo_unit(i * 2 + 4, 0, acc[1])
                wo_unit(i * 2 + 5, 1, acc[0])

            def up_step(i, first):
                if not first:
                    st.loop(i, 1, UP_DVE_STEPS)
                for s in range(UP_TILES):
                    split_lo(i * UP_TILES + (T_UP + s + LEAD), (s + LEAD) % RING)
                    if first and s == 1:
                        dve.wait_ge(y2_root, 1)
                        dve.reciprocal(r2b[:], ysq[:, 0]).then_inc(r2_s, 1)
                        dve.wait_ge(r2_s, 1)
                    if first and s == 2:
                        st.done(dve.memset(ub[:, :, :, 0:2], 0.0))
                        st.wait()
                    if s in (3, 7):
                        v = s // 4
                        bank = acc[2] if v == 0 else acc[1]
                        dve.wait_ge(mm_done, i * UP_TILES + (T_UP + s + 1))
                        for b in range(2):
                            dve.tensor_tensor(ub[:, v, b, 2:S + 2], bank[:, b * S:(b + 1) * S], r2b[:],
                                              ALU.mult).then_inc(u_s, 1)
                        for b in range(2):
                            dve.wait_ge(c0_s, i * 4 + (2 * v + b + 1))
                            st.done(dve.scalar_tensor_tensor(conv_o[:, v, b], ub[:, v, b, 1:S + 1],
                                                             tap(1, i * 2 + (b + v * FB)), conv_o[:, v, b],
                                                             ALU.mult, ALU.add))
                        for b in range(2):
                            if b == 0:
                                st.wait()
                            dve.scalar_tensor_tensor(conv_o[:, v, b], ub[:, v, b, 0:S], tap(0, i * 2 + (b + v * FB)),
                                                     conv_o[:, v, b], ALU.mult, ALU.add).then_inc(conv_s, 1)
                    if s == 7:
                        dve.wait_ge(silu_s, i + 1)
                        for b in range(2):
                            dve.wait_ge(conv_s, i * 4 + (b + 3))
                            dve.tensor_tensor(silu[:, b], silu[:, b], conv_o[:, 1, b], ALU.mult).then_inc(gated_s, 1)
                        for b in range(2):
                            dve.wait_ge(ghi_s, i * 2 + (b + 1))
                            ins = dve.tensor_tensor(g_lo[:, bass.ds(i * 2 + b, 1), :].rearrange("p a n -> p (a n)"),
                                                    silu[:, b],
                                                    g_hi[:, bass.ds(i * 2 + b, 1), :].rearrange("p a n -> p (a n)").bitcast(F32),
                                                    ALU.subtract)
                        ins.then_inc(glo_s, 1)
                if not first:
                    st.end(UP_STEPS)

            up_step(0, True)
            with dve.Fori(1, UP_STEPS) as i:
                up_step(i, False)

            def make_z(n, tiles):
                bank = sc_ps if n % 2 == 0 else tr_ps
                for m in tiles:
                    dve.tensor_tensor(nat[:, m, n * 512:(n + 1) * 512], bank[:, m],
                                      nat[:, m, n * 512:(n + 1) * 512], ALU.add).then_inc(z_s, 1)

            def gain(n):
                dve.wait_ge(zsq_s, n + 1)
                for m in range(MT):
                    ins = dve.tensor_tensor(nat[:, m, n * 512:(n + 1) * 512], nat[:, m, n * 512:(n + 1) * 512],
                                            gfin[:, n * 512:(n + 1) * 512], ALU.mult)
                ins.then_inc(z_rms, 1)

            for t in range(GROUPS * DOWN_TILES):
                if T_DOWN + t + LEAD < T_END:
                    split_lo(T_DOWN + t + LEAD, (t + LEAD) % RING)
                n, kt = divmod(t, DOWN_TILES)
                if t == 0:
                    dve.wait_ge(ynat_s, WO_UNITS)
                if kt == DOWN_TILES - 1 and n < 3:
                    dve.wait_ge(mm_done, T_DOWN + t + 1)
                    make_z(n, range(MT))
                if kt == 4 and n > 0:
                    if n == 1:
                        dve.wait_ge(d_gf, 16)
                    gain(n - 1)
                if kt == 5 and n == 3:
                    dve.tensor_reduce(small[:, 26:28], ss3[:, :, 0:3], AX.X, ALU.add).then_inc(z_tot, 1)
                    dve.wait_ge(z_tot, 1)
                    dve.tensor_scalar(part3, small[:, 26:28], 1.0 / D, EPS, ALU.mult, ALU.add).then_inc(part_s, 1)
            for m in range(MT):
                dve.wait_ge(last_s, m + 1)
                make_z(3, [m])
                dve.wait_ge(z_root, m + 1)
                dve.reciprocal(r3[:, m:m + 1], root3[:, m:m + 1]).then_inc(z_rms, 1)
                dve.wait_ge(z_rms, m + 4)
                dve.tensor_scalar(nat[:, m, OUT_CUTS[1]:OUT_CUTS[2]], nat[:, m, OUT_CUTS[1]:OUT_CUTS[2]], r3[:, m:m + 1], None,
                                  ALU.mult).then_inc(fin_d, 1)
                dve.scalar_tensor_tensor(nat[:, m, OUT_CUTS[2]:D], nat[:, m, OUT_CUTS[2]:D], r3[:, m:m + 1],
                                         gfin[:, OUT_CUTS[2]:D], ALU.mult, ALU.mult).then_inc(fin_d, 1)

        @block.tensor
        def _(pe):
            pe.wait_ge(ones_s, 1)
            for n in range(WARM):
                pe.matmul(tr_ps[:, 0, 0:P], ones[:], ones[:], start=True, stop=True)
            pe.wait_ge(d_id, 16)
            pe.wait_ge(d_nrm, 32)
            pe.transpose(pv_ps[:, 0:2 * KB], rows[0:2 * KB, 0, :], ident[0:2 * KB, 0:2 * KB]).then_inc(cst_t, 1)

            def turn_x_pair(pr):
                pe.wait_ge(d_x[pr // 2], 32)
                if pr == 7:
                    pe.wait_ge(cst_c, 1)
                for b in range(2):
                    for m in range(MT):
                        o = b * S + m * P
                        c = 2 * pr + b
                        ins = pe.transpose(x_banks[pr][:, o:o + P], nat[:, m, c * P:(c + 1) * P], ident[:])
                ins.then_inc(x_t, 1)

            for pr in range(4):
                turn_x_pair(pr)
            for n in range(WARM_AGAIN):
                pe.matmul(tr_ps[:, 0, 0:P], ones[:], ones[:], start=True, stop=True)

            def mm3(dst, a_hi, a_lo, b_hi, b_lo, start=False):
                pe.matmul(dst, a_hi, b_hi, start=start, stop=False, skip_group_check=True)
                pe.matmul(dst, a_hi, b_lo, start=False, stop=False, skip_group_check=True)
                return pe.matmul(dst, a_lo, b_hi, start=False, stop=True, skip_group_check=True)

            def features(t, slot, bank, kt, a_hi, a_lo, first):
                pe.wait_ge(lo_done, t + 1)
                wh, wl = narrow(hi, slot), narrow(lo, slot)
                for c in range(4):
                    for b in range(2):
                        ins = mm3(bank[:, b * S:(b + 1) * S], wh[:, c, b * P:(b + 1) * P], wl[:, c, b * P:(b + 1) * P],
                                  a_hi[:, 4 * kt + c], a_lo[:, 4 * kt + c], start=first and c == 0 and b == 0)
                ins.then_inc(mm_done, 1)

            def tokens(t, slot, bank, kt, first):
                pe.wait_ge(lo_done, t + 1)
                wh, wl = narrow(hi, slot), narrow(lo, slot)
                for c in range(4):
                    for m in range(MT):
                        k = 4 * kt + c
                        ins = mm3(bank[:, m * S:(m + 1) * S], act_hi[:, k, m * P:(m + 1) * P],
                                  act_lo[:, k, m * P:(m + 1) * P], wh[:, c], wl[:, c],
                                  start=first and c == 0 and m == 0)
                ins.then_inc(mm_done, 1)

            for kt in range(4):
                pe.wait_ge(lo_done, kt + 1)
                wh, wl = with_gates(hi, kt), with_gates(lo, kt)
                for c in range(4):
                    k = 4 * kt + c
                    pe.wait_ge(xlo, k + 1 if k else 4)
                    for m, bank in enumerate((acc[0], acc[2])):
                        ins = mm3(bank[:, 0:VA_COLS], act_hi[:, k, m * P:(m + 1) * P],
                                  act_lo[:, k, m * P:(m + 1) * P], wh[:, c], wl[:, c], start=k == 0)
                ins.then_inc(mm_done, 1)
                if kt == 0:
                    for pr in range(4, 8):
                        turn_x_pair(pr)
            for kt in range(4):
                features(T_KA + kt, kt, acc[1], kt, act_hi, act_lo, kt == 0)
                if kt == 2:
                    pe.wait_ge(ones_s, 1)
                    pe.wait_ge(diag_done, 2)
                    for m in range(MT):
                        ins = pe.matmul(sc_ps[:, 0, m * P:(m + 1) * P], ones[:], diag[:, m], start=True, stop=True)
                    ins.then_inc(rms1_ps, 1)
                if kt == 3:
                    pe.wait_ge(nlf_s, 2)
                    pe.wait_ge(tri_s, 1)
                    for m in range(MT):
                        for k in range(m + 1):
                            t0 = 0 if k == m else P
                            for n, part in enumerate((nlf_hi, nlf_lo)):
                                ins = pe.matmul(pv_ps[:, m * NH:(m + 1) * NH], tri[:, t0:t0 + P], part[:, k],
                                                start=m == 0 and k == 0 and n == 0, stop=True, skip_group_check=True)
                    ins.then_inc(fcum_ps, 1)
            def attention(s, slots, q):
                for e in slots.get(s, []):
                    p = int(e[1])
                    if e[0] == "S":
                        if p == 0:
                            pe.wait_ge(quad_s, q + 1)
                            pe.wait_ge(evac_a, q + 2)
                            pe.wait_ge(evac_d, q * 3 + 4)
                        pe.wait_ge(read_s, q * 4 + (p + 1))
                        for c0, c1, qs, n in ((0, 128, 0, 128), (128, 384, 128, 256)):
                            for h in range(2):
                                half = slice(h * HD, (h + 1) * HD)
                                qv, kv = (qa[half, p], kq[half]) if p < 2 else (qf[half, p - 2], kf[half, p - 2])
                                ins = pe.matmul(sc_ps[:, h, c0:c1], qv[:, qs:qs + 128], kv[:, 0:n], start=c0 == 0,
                                                stop=True, skip_group_check=True)
                        ins.then_inc(scores_s, 1)
                    if e[0] == "T":
                        pe.wait_ge(prob_s, q * 4 + (p + 1))
                        for h in range(2):
                            for c in range(3):
                                ins = pe.transpose(tr_ps[:, h, c * P:(c + 1) * P], prob[:, p, h, c * P:(c + 1) * P], ident[:])
                        ins.then_inc(pt_ps, 1)
                    if e[0] == "V":
                        pe.wait_ge(pt_s, q * 4 + (p + 1))
                        pe.wait_ge(mixlo_s, q * 4 + (p + 1))
                        for h in range(2):
                            i = (p - 2) * 2 + h
                            v = vq[:] if p < 2 else vf[:, :, i * HD:(i + 1) * HD]
                            half = slice(h * HD, (h + 1) * HD)
                            pe.matmul(pv_ps[half, 0:S], v[:, 0], prob_t[:, p % 2, h, 0:S], start=True, stop=False,
                                      skip_group_check=True)
                            ins = pe.matmul(pv_ps[half, P:S], v[:, 1], prob_t[:, p % 2, h, S:384], start=False, stop=True,
                                            skip_group_check=True)
                        ins.then_inc(pv_s, 1)

            def quad(j, attend):
                for s in range(QUAD_TILES):
                    n, kt = divmod(s, 4)
                    if kt == 0:
                        if n == 0:
                            if attend:
                                pe.wait_ge(evac_d, j * 3 + 1)
                            else:
                                pe.wait_ge(evac_a, 1)
                        if n == 1:
                            if attend:
                                pe.wait_ge(evac_a, j + 1)
                            else:
                                pe.wait_ge(swap_s, 1)
                                pe.wait_ge(evac_d, 1)
                        if n == 2:
                            pe.wait_ge(swap_s, j + 2)
                            pe.wait_ge(evac_d, j * 3 + 2)
                        if n == 3:
                            pe.wait_ge(evac_d, j * 3 + 3)
                    t = j * QUAD_TILES + (T_QUAD + s)
                    if n < 3:
                        features(t, kt, acc[n % 2], kt, act_hi, act_lo, kt == 0)
                    else:
                        tokens(t, kt, acc[1], kt, kt == 0)
                    if attend:
                        attention(s, SLOTS_LOOP, j - 1)
                    elif s == 1:
                        for n, c0, c1 in ((0, 0, S), (1, P, S)):
                            ins = pe.matmul(sc_ps[0:NH, 1, c0:c1], fg[:, 5, n], tri_f[:, 0:c1 - c0], start=n == 0,
                                            stop=n == 1, skip_group_check=True)
                        ins.then_inc(nft_ps, 1)
                        pe.wait_ge(d_cnv, 64)
                        pe.wait_ge(fcum_s, 1)
                        for k in range(4):
                            ins = pe.transpose(pv_ps[:, 128 + 88 * k:216 + 88 * k], rows[0:88, 1 + k, :], ident[0:88, 0:88])
                        ins.then_inc(cst_t, 1)

            quad(0, False)
            with pe.Fori(1, QUADS) as j:
                quad(j, True)

            def turn_x(u):
                pe.wait_ge(xcols_s, u + 1)
                for b in range(2):
                    for m in range(MT):
                        ins = pe.transpose(sc_ps[:, 0, b * S + m * P:b * S + (m + 1) * P],
                                           xcols[:, m, b * P:(b + 1) * P], ident[:])
                ins.then_inc(xt_ps, 1)

            def turn_y(u, par):
                pe.wait_ge(yt_s, u + 1)
                if not (isinstance(u, int) and u == 0):
                    pe.wait_ge(ynat_s, u)
                for m in range(MT):
                    for b in range(2):
                        ins = pe.transpose(sc_ps[:, 1, m * S + b * P:m * S + (b + 1) * P],
                                           yt[:, par, b, m * P:(m + 1) * P], ident[:])
                ins.then_inc(yt_ps, 1)

            for s, (u, kt) in enumerate(WOA_ORDER):
                if s == 0:
                    pe.wait_ge(evac_d, 3 * QUADS + 1)
                if s == 1:
                    pe.wait_ge(evac_a, QUADS + 1)
                if s == 6:
                    pe.wait_ge(mixlo_s, 4 * (QUADS - 1) + 3)
                if s == 9:
                    pe.wait_ge(mixlo_s, 4 * QUADS + 1)
                features(T_WOA + s, s % RING, acc[u], kt, mix_hi, mix_lo, kt == 0)
                attention(s, SLOTS_TAIL, QUADS - 1)
                if 8 <= s < 11:
                    if s == 8:
                        pe.wait_ge(read_s, 4 * QUADS + 1)
                    else:
                        pe.wait_ge(xts_s, s - 8)
                    turn_x(s - 8)
                if s >= 10:
                    turn_y(s - 10, s % 2)

            def wo_unit(u, par, bank, free):
                pe.wait_ge(yt_s, free)
                for s in range(4):
                    features(u * 4 + (T_WOB - 4 * WOA_UNITS + s), s, bank, s, mix_hi, mix_lo, s == 0)
                    if s == 0:
                        turn_y(u - 1, 1 - par)
                    if s == 2:
                        pe.wait_ge(xts_s, u)
                        turn_x(u)

            wo_unit(WOA_UNITS, WOA_UNITS % 2, acc[0], 1)
            with pe.Fori(0, 2) as i:
                wo_unit(i * 2 + 4, 0, acc[1], i * 2 + 3)
                wo_unit(i * 2 + 5, 1, acc[0], i * 2 + 4)

            def up_step(i, first):
                for s in range(UP_TILES):
                    v, kt = divmod(s, 4)
                    if kt == 0:
                        if first:
                            pe.wait_ge(yt_s, WO_UNITS - 1)
                        else:
                            pe.wait_ge(u_s, i * 4 + (2 * v - 2))
                    if first and v == 0:
                        pe.wait_ge(ylo_s, 2 * kt + 2)
                    features(i * UP_TILES + (T_UP + s), kt, acc[2 - v], kt, act_hi, act_lo, kt == 0)
                    if first and s == 0:
                        turn_y(WO_UNITS - 1, 1)
                        pe.wait_ge(ysum_s, WO_UNITS)
                        for b in range(2):
                            ins = pe.matmul(pv_ps[:, 0:S], ones[:], ysum[:, b], start=b == 0, stop=b == 1)
                        ins.then_inc(y2_ps, 1)

            up_step(0, True)
            with pe.Fori(1, UP_STEPS) as i:
                up_step(i, False)

            pe.wait_ge(ynat_s, WO_UNITS)

            def down(n, kt, tiles):
                bank = sc_ps if n % 2 == 0 else tr_ps
                slot = (n * DOWN_TILES + kt) % RING
                wh, wl = wide(hi, slot), wide(lo, slot)
                for c in range(2):
                    for m in tiles:
                        b = 2 * kt + c
                        ins = mm3(bank[:, m], g_hi[:, b, m * P:(m + 1) * P], g_lo[:, b, m * P:(m + 1) * P],
                                  wh[:, c], wl[:, c], start=kt == 0 and c == 0)
                return ins

            for n in range(GROUPS):
                for kt in range(DOWN_TILES - (LAST if n == 3 else 0)):
                    if n == 0:
                        pe.wait_ge(glo_s, kt + 1)
                    if kt == 0:
                        pe.wait_ge(z_s, 2 * n + 2)
                    pe.wait_ge(lo_done, T_DOWN + n * DOWN_TILES + kt + 1)
                    down(n, kt, range(MT)).then_inc(mm_done, 1)
            for m in range(MT):
                for kt in range(DOWN_TILES - LAST, DOWN_TILES):
                    if m == 0:
                        pe.wait_ge(lo_done, T_DOWN + 3 * DOWN_TILES + kt + 1)
                    ins = down(3, kt, [m])
                ins.then_inc(last_s, 1)


def constants():
    pos = np.arange(S)
    inv = (1.0 / (np.float32(10000.0) ** (np.arange(HD // 2, dtype=np.float32) * np.float32(2.0 / HD)))).astype(np.float32)
    ang = (pos.astype(np.float32)[None, :] * inv[:, None]).astype(np.float32)
    cos, sin = np.cos(ang).astype(np.float32), np.sin(ang).astype(np.float32)
    tri = np.triu(np.ones((P, P), np.float32))
    q, k = np.arange(P)[:, None], np.arange(S)[None, :]

    def mask(valid):
        both = np.concatenate([valid(q, k[:, :P]), valid(q + P, k)], axis=1)
        return np.where(both, 0.0, -1e30).astype(np.float32)

    return {
        "ident_c": np.eye(P, dtype=np.float32),
        "tri_c": np.concatenate([tri, np.ones((P, P), np.float32)], axis=1),
        "mask_a_c": mask(lambda q, k: (q // 64 - k // 64 >= 0) & (q // 64 - k // 64 <= 1)),
        "mask_b_c": mask(lambda q, k: k <= q)[:, :P].copy(),
        "cos_c": np.concatenate([cos] * 4),
        "sin_c": np.concatenate([-sin, sin] * 2),
    }


NAMES = ("x", "norm_mix", "w_in", "sinks", "b_f", "w_o", "norm_ffn", "w_up", "conv_w", "conv_b", "w_down", "norm_final")


def kernel(**inputs):
    import concourse.bacc as bacc
    from concourse.bass_utils import run_bass_kernel_spmd

    nc = bacc.Bacc("TRN2", target_bir_lowering=False, num_devices=1)
    arrays = {name: np.ascontiguousarray(inputs[name]) for name in NAMES}
    arrays.update(constants())
    args = [nc.dram_tensor(name, a.shape, mybir.dt.from_np(a.dtype), kind="ExternalInput").ap()
            for name, a in arrays.items()]
    result = nc.dram_tensor("result", (1, S, D), F32, kind="ExternalOutput").ap()
    program(nc, *args, result)
    return run_bass_kernel_spmd(nc, [arrays], core_ids=[0]).results[0]["result"]
```

```python
import numpy as np
import concourse.bass as bass
from concourse import mybir
from contextlib import ExitStack

F32 = mybir.dt.float32
R32 = mybir.dt.float32r
ALU = mybir.AluOpType
ACT = mybir.ActivationFunctionType
AX = mybir.AxisListType

P = 128
D = 2048
S = 256
KB = D // P
MT = S // P
HD = 64
NKV = 4
NH = 16
F = 5632
FB = F // P
EPS = 1e-5
QSCALE = HD ** -0.5
COL_QA, COL_KA, COL_VA = 0, 1024, 1280
COL_QF, COL_KF, COL_VF, COL_F = 1536, 2560, 3584, 4608

RING = 4
WARM = 8
WARM_AGAIN = (6, 3)
LEAD = 3
TILE = 1024
VA_COLS = 256 + NH
SLOT = 4 * VA_COLS
QUADS = 4
UP_STEPS = FB // 2
QUAD_STEPS = 13
UP_DVE_STEPS = 8
GROUPS = D // 512
LG = GROUPS - 1
LG_COL = LG * 512
DOWN_TILES = FB // 2

T_KA = 4
T_QUAD = 8
QUAD_TILES = 16
T_WOA = T_QUAD + QUADS * QUAD_TILES
WOA_UNITS = 3
T_WOB = T_WOA + 4 * WOA_UNITS
WO_UNITS = 8
T_UP = T_WOB + 4 * (WO_UNITS - WOA_UNITS)
UP_TILES = 8
T_DOWN = T_UP + UP_STEPS * UP_TILES
OUT_CUTS = (0, 512, 1024, 1536, D)
UP_SPLITS = [[], [4], [5], [6], [], [8], [9], [10]]
LAST = RING
T_END = T_DOWN + GROUPS * DOWN_TILES
WOA_ORDER = [(0, 0), (1, 0), (2, 0), (0, 2), (1, 2), (2, 2), (0, 1), (1, 1), (0, 3), (2, 1), (1, 3), (2, 3)]
WOA_END = [8, 10, 11]
WOA_X = [7, 9, 10]
WOA_Y = [9, 11]

SLOTS_OWN = {11: ["S0"], 13: ["S1"], 14: ["T0"], 15: ["V0"]}
SLOTS_PREV = {0: ["T1"], 1: ["V1"], 2: ["S2"], 5: ["T2"], 6: ["V2", "S3"], 9: ["T3"], 10: ["V3"]}
SLOTS_TAIL = {0: ["T1", "S2"], 1: ["V1"], 2: ["S3"], 3: ["T2"], 4: ["V2"], 5: ["T3"], 6: ["V3"]}
X_THEN = [3, 7, 11]
BIAS_SLOTS = [7, 8, 9, 10]


def at_slot(slots, s, kind):
    return [int(e[1]) for e in slots.get(s, []) if e[0] == kind]


class Steps:

    def __init__(self, eng, sem):
        self.eng, self.sem, self.base, self.k, self.i, self.per = eng, sem, 0, 0, 0, 0

    def loop(self, i, first, per):
        self.base, self.k = self.base + self.k - first * per, 0
        self.i, self.per = i, per

    def end(self, passes_end):
        assert self.k == self.per, f"steps per pass: {self.k}"
        self.base, self.k, self.i, self.per = self.base + passes_end * self.per, 0, 0, 0

    def done(self, ins):
        ins.then_inc(self.sem, 1)
        self.k += 1

    def wait(self):
        self.eng.wait_ge(self.sem, self.i * self.per + (self.base + self.k))


class Sbuf:

    def __init__(self, nc):
        self.nc, self.cursor = nc, (nc.sbuf_base + 63) // 64 * 64

    def place(self, name, shape, dt=F32):
        t = self.nc.alloc_sbuf_tensor_at(name, shape, dt, offset=self.cursor)
        self.cursor += (4 * int(np.prod(shape[1:])) + 31) // 32 * 32
        return t


def program(nc, x, norm_mix, w_in, sinks, b_f, w_o, norm_ffn, w_up, conv_w, conv_b, w_down, norm_final,
            ident_c, tri_c, mask_a_c, mask_b_c, cos_c, sin_c, out):
    ctx = ExitStack()
    with ctx:
        sbuf = Sbuf(nc)
        sb = sbuf.place

        def ps(name, shape):
            return ctx.enter_context(nc.psum_tensor(name, shape, F32))

        def sem(name):
            return ctx.enter_context(nc.semaphore(name))

        raw = sb("raw", [P, RING, SLOT])
        hi = sb("hi", [P, RING, SLOT], R32)
        lo = sb("lo", [P, RING, SLOT], R32)
        nat = sb("nat", [P, MT, D])
        act_at = sbuf.cursor
        act_split = sb("act_split", [P, 2, KB, S], R32)
        act_hi, act_lo = act_split[:, 0], act_split[:, 1]
        ident = sb("ident", [P, P])
        ones = sb("ones", [P, P])
        cst = sb("cst", [P, 384])
        r2b = sb("r2b", [P, S])
        small = sb("small", [P, 96])

        region = sbuf.cursor
        g_hi = sb("g_hi", [P, FB, S], R32)
        g_lo = sb("g_lo", [P, FB, S], R32)
        region_end = sbuf.cursor
        sbuf.cursor = region
        mix_hi = sb("mix_hi", [P, KB, S], R32)
        mix_lo = sb("mix_lo", [P, KB, S], R32)
        va = sb("va", [P, MT, S])
        kta = sb("kta", [P, NKV, S])
        kq = sb("kq", [P, S])
        vq = sb("vq", [P, MT, HD])
        qa = sb("qa", [P, 2, S])
        kf = sb("kf", [P, 2, S])
        qf = sb("qf", [P, 2, S])
        vf = sb("vf", [P, MT, S])
        prob = sb("prob", [P, 4, 2, 384])
        prob_t = sb("prob_t", [P, 2, 2, 384])
        cos_r = sb("cos_r", [P, S])
        sin_r = sb("sin_r", [P, S])
        swap = sb("swap", [P, 2, S])
        rope_a = sb("rope_a", [P, 2, S])
        r1b = sb("r1b", [P, S])
        mask_a = sb("mask_a", [P, 384])
        mask_b = sb("mask_b", [P, P])
        fg = sb("fg", [P, 8, MT, NH])
        nlf_hi = sb("nlf_hi", [P, MT, NH], R32)
        nlf_lo = sb("nlf_lo", [P, MT, NH], R32)
        nft = sb("nft", [NH, S])
        fcum = sb("fcum", [P, MT, NH])
        fq = sb("fq", [P, MT, 4])
        nsink = sb("nsink", [P, MT, NH])
        nsq = sb("nsq", [P, MT, 4])
        stat = sb("stat", [P, 4, 5, 4])
        bf_b = sb("bf_b", [P, NH])
        key_bias_at = sbuf.cursor
        cos_t = sb("cos_t", [P, S])
        sin_t = sb("sin_t", [P, S])
        rope_b = sb("rope_b", [P, 2, S])
        diag = sb("diag", [P, MT, P])
        tri_f = sb("tri_f", [P, S])
        tri = sb("tri", [P, S], R32)
        sbuf.cursor = key_bias_at
        key_bias = sb("key_bias", [P, NH, 384])

        assert key_bias_at <= region_end and sbuf.cursor <= nc.sbuf_usable_end
        sbuf.cursor = region_end
        ub = sb("ub", [P, 2, 2, S + 2])
        conv_o = sb("conv_o", [P, 2, 2, S])
        silu = sb("silu", [P, 2, S])
        up_r = sb("up_r", [P, 2, S])
        top = sbuf.cursor
        sbuf.cursor = region_end
        xts = sb("xts", [P, 2, S])
        yt = sb("yt", [P, 2, 2, S])
        ysq = sb("ysq", [P, 2, S])
        ysum = sb("ysum", [P, 2, S])
        xcols = sb("xcols", [P, MT, 2 * P])
        assert max(top, sbuf.cursor) <= nc.sbuf_usable_end
        sbuf.cursor = act_at
        gfin = sb("gfin", [P, D])
        sq_out = sb("sq_out", [P, MT, 512])
        z_gain = sb("z_gain", [P, MT, 512])

        acc = [ps(f"acc{i}", [P, 512]) for i in range(3)]
        sc_ps = ps("sc_ps", [P, 2, 512])
        tr_ps = ps("tr_ps", [P, 2, 512])
        pv_ps = ps("pv_ps", [P, 512])
        x_banks = [acc[0][:], acc[2][:], acc[1][:], sc_ps[:, 0], sc_ps[:, 1], tr_ps[:, 0], tr_ps[:, 1], pv_ps[:]]

        up_banks = [[tr_ps[:, 0], tr_ps[:, 1]], [acc[1][:], acc[2][:]]]

        d_w = [sem(f"d_w{i}") for i in range(RING)]
        d_x = [sem(f"d_x{i}") for i in range(4)]
        d_bias = [sem(f"d_bias{i}") for i in range(4)]
        d_id, d_nrm, d_cnv, d_cst, d_tab, d_gf, d_out = (sem(n) for n in (
            "d_id", "d_nrm", "d_cnv", "d_cst", "d_tab", "d_gf", "d_out"))
        hi_done, lo_done, mm_done = sem("hi_done"), sem("lo_done"), sem("mm_done")
        act_step, dve_step = sem("act_step"), sem("dve_step")
        cst_t, cst_c = sem("cst_t"), sem("cst_c")
        x_t, xhi, xlo = sem("x_t"), sem("xhi"), sem("xlo")
        evac_d, evac_a = sem("evac_d"), sem("evac_a")
        ones_s = sem("ones_s")
        rms1_root, rms1_done, diag_done, rms1_ps, r1b_done = (sem(n) for n in (
            "rms1_root", "rms1_done", "diag_done", "rms1_ps", "r1b_done"))
        f_abs, f_ln, nlf_s, fcum_ps, fcum_s, nft_ps, nft_s, nft_out, bias_s = (sem(n) for n in (
            "f_abs", "f_ln", "nlf_s", "fcum_ps", "fcum_s", "nft_ps", "nft_s", "nft_out",
            "bias_s"))
        tri_s, kta_s, swap_s, krope_s, nsink_s, quad_s, fq_s = (sem(n) for n in (
            "tri_s", "kta_s", "swap_s", "krope_s", "nsink_s", "quad_s", "fq_s"))
        scores_s, read_s, negmax_s, exp_s, prob_s, pt_ps, pt_s, pv_s, mixhi_s, mixlo_s = (sem(n) for n in (
            "scores_s", "read_s", "negmax_s", "exp_s", "prob_s", "pt_ps", "pt_s", "pv_s", "mixhi_s", "mixlo_s"))
        xcols_s, xt_ps, xts_s, yt_s, ysq_s, yhi_s, ylo_s, yt_ps, ynat_s, ysum_s, y2_ps, y2_root, r2_s = (sem(n) for n in (
            "xcols_s", "xt_ps", "xts_s", "yt_s", "ysq_s", "yhi_s", "ylo_s", "yt_ps", "ynat_s", "ysum_s", "y2_ps",
            "y2_root", "r2_s"))
        pad_s, upr_s, u_s, c0_s, conv_s, silu_s, gated_s, ghi_s, glo_s = (sem(n) for n in (
            "pad_s", "upr_s", "u_s", "c0_s", "conv_s", "silu_s", "gated_s", "ghi_s", "glo_s"))
        z_s, zsq_s, z_tot, z_root, z_rms, fin_a, fin_d, part_s, last_s = (sem(n) for n in (
            "z_s", "zsq_s", "z_tot", "z_root", "z_rms", "fin_a", "fin_d", "part_s", "last_s"))

        nft_dram = nc.dram_tensor("nft_dram", (NH, S), F32).ap()

        win = w_in[0].rearrange("(t c p) n -> t p c n", p=P, c=4)
        wo = w_o[0].rearrange("(t c p) n -> t p c n", p=P, c=4)
        wup = w_up[0].rearrange("(t c p) n -> t p c n", p=P, c=4)
        wdn = w_down[0].rearrange("(t c p) n -> t p c n", p=P, c=2)

        def narrow(t, slot):
            return t[:, slot, 0:TILE].rearrange("p (c n) -> p c n", c=4)

        def wide(t, slot):
            return t[:, slot, 0:TILE].rearrange("p (c n) -> p c n", c=2)

        def with_gates(t, slot):
            return t[:, slot].rearrange("p (c n) -> p c n", c=4)

        flat = prob[:].rearrange("p a b n -> p (a b n)")
        rows = flat[:, D:D + 5 * P].rearrange("p (j n) -> p j n", j=5)
        eps = small[:, 0:1]
        ss1 = small[:, 2:4]
        root1 = small[:, 4:6]
        r1c = small[:, 6:8]
        ss3 = small[:, 8:16].rearrange("p (m g) -> p m g", m=2)
        part3 = small[:, 16:18]
        root3 = small[:, 18:20]
        r3 = small[:, 20:22]
        g1 = cst[:, 0:KB]
        g2 = cst[:, KB:2 * KB]

        def tap(j, b, n=1):
            return cst[:, bass.ds(32 + 88 * j + b, n)]

        block = ctx.enter_context(nc.Block())

        @block.sync
        def _(sp):
            def load_x(c):
                for m in range(MT):
                    sp.dma_start(nat[:, m, c * 512:(c + 1) * 512],
                                 x[0, m * P:(m + 1) * P, c * 512:(c + 1) * 512]).then_inc(d_x[c], 16)

            load_x(0)
            sp.dma_start(rows[0:KB, 0], norm_mix.rearrange("a (b p) -> (a b) p", p=P)).then_inc(d_nrm, 16)
            for c in range(4):
                if c == 1:
                    load_x(1)
                    load_x(2)
                if c == 2:
                    load_x(3)
                sp.dma_start(with_gates(raw, c)[:, :, 0:256], win[c][:, :, COL_VA:COL_VA + 256]).then_inc(d_w[c], 16)
                sp.dma_start(with_gates(raw, c)[:, :, 256:VA_COLS], win[c][:, :, COL_F:COL_F + NH]).then_inc(d_w[c], 16)

            def load(t, slot, dst, src):
                sp.wait_ge(lo_done, t - (RING - 1))
                sp.dma_start(dst, src).then_inc(d_w[slot], 16)

            def load_unit(t, w, col, kts=range(4)):
                for k, kt in enumerate(kts):
                    load(t + k, k, narrow(raw, k), w[kt][:, :, bass.ds(col, 256)])

            load_unit(T_KA, win, COL_KA, range(2))
            for dst, src in ((cos_t[:], cos_c), (sin_t[:], sin_c), (tri_f[:], tri_c), (mask_a[:], mask_a_c),
                             (mask_b[:], mask_b_c)):
                sp.dma_start(dst, src).then_inc(d_tab, 16)
            for k in range(2, 4):
                load(T_KA + k, k, narrow(raw, k), win[k][:, :, COL_KA:COL_KA + 256])
            with sp.Fori(0, QUADS) as j:
                for n, col in enumerate((COL_QA, COL_KF, COL_QF, COL_VF)):
                    load_unit(j * QUAD_TILES + (T_QUAD + 4 * n), win, j * 256 + col)
            for n, (u, kt) in enumerate(WOA_ORDER):
                load(T_WOA + n, n % RING, narrow(raw, n % RING), wo[kt][:, :, u * 256:(u + 1) * 256])
            with sp.Fori(0, WO_UNITS - WOA_UNITS) as u:
                load_unit(u * 4 + T_WOB, wo, u * 256 + WOA_UNITS * 256)
            with sp.Fori(0, UP_STEPS) as i:
                load_unit(i * UP_TILES + T_UP, wup, i * 256)
                load_unit(i * UP_TILES + (T_UP + 4), wup, i * 256 + F)
            with sp.Fori(0, GROUPS // 2) as g:
                for k in range(2 * DOWN_TILES):
                    n, kt = divmod(k, DOWN_TILES)
                    load(g * (2 * DOWN_TILES) + (T_DOWN + k), k % RING, wide(raw, k % RING),
                         wdn[kt][:, :, bass.ds(g * 1024 + n * 512, 512)])
            for m in range(MT):
                for k in (1, 0, 2, 3):
                    if k == 0 and m == 1:
                        continue
                    if k == 0:
                        sp.wait_ge(fin_a, 1)
                    else:
                        sp.wait_ge(fin_d, 3 * m + k)
                    cols = slice(OUT_CUTS[k], OUT_CUTS[k + 1])
                    sp.dma_start(out[0, m * P:(m + 1) * P, cols], nat[:, m, cols]).then_inc(d_out, 16)
            sp.wait_ge(d_out, 128)

        @block.gpsimd
        def _(pool):
            pool.memset(ones[:], 1.0).then_inc(ones_s, 1)
            for j in range(3):
                pool.dma_start(rows[0:2 * FB, 1 + j], conv_w[0, j].rearrange("(b p) -> b p", p=P)).then_inc(d_cnv, 16)
            pool.dma_start(rows[0:2 * FB, 4], conv_b.rearrange("a (b p) -> (a b) p", p=P)).then_inc(d_cnv, 16)
            for dst, src in ((nsink[:, 0], sinks[0].partition_broadcast(P)),
                             (nsink[:, 1], sinks[0].partition_broadcast(P)), (bf_b[:], b_f[0].partition_broadcast(P))):
                pool.dma_start(dst, src).then_inc(d_cst, 16)
            for c in range(4):
                pool.wait_ge(d_x[c], 32)
            pool.wait_ge(kta_s, 4)
            pool.wait_ge(evac_a, 1)
            pool.wait_ge(nlf_s, 2)
            pool.wait_ge(fcum_s, 1)
            pool.wait_ge(nsink_s, 1)

            def copy_group_a(j):
                pool.tensor_copy(kq[:], kta[:, bass.ds(j, 1), :].rearrange("p a n -> p (a n)"))
                pool.tensor_copy(vq[:], va[:, :, bass.ds(j * HD, HD)])
                pool.tensor_copy(nsq[:], nsink[:, :, bass.ds(j * 4, 4)]).then_inc(quad_s, 1)

            copy_group_a(0)
            pool.tensor_copy(fq[:], fcum[:, :, 0:4]).then_inc(fq_s, 1)
            pool.wait_ge(nft_s, 1)
            pool.dma_start(nft_dram, nft[:]).then_inc(nft_out, 16)
            pool.wait_ge(nft_out, 16)
            for n in range(4):
                pool.dma_start(key_bias[:, 4 * n:4 * n + 4, P:384],
                               nft_dram[4 * n:4 * n + 4].partition_broadcast(P)).then_inc(d_bias[n], 16)
            with pool.Fori(1, QUADS) as j:
                pool.wait_ge(mixlo_s, j * 4 - 1)
                copy_group_a(j)
                pool.wait_ge(mixlo_s, j * 4 + 1)
                pool.tensor_copy(fq[:], fcum[:, :, bass.ds(j * 4, 4)]).then_inc(fq_s, 1)
            pool.wait_ge(read_s, 4 * QUADS + 1)
            pool.tensor_copy(xcols[:], nat[:, :, 0:2 * P]).then_inc(xcols_s, 1)
            with pool.Fori(1, WO_UNITS) as u:
                pool.wait_ge(xt_ps, u)
                pool.tensor_copy(xcols[:], nat[:, :, bass.ds(u * 2 * P, 2 * P)]).then_inc(xcols_s, 1)
            pool.wait_ge(mm_done, T_DOWN)
            pool.dma_start(gfin[:], norm_final.partition_broadcast(P)).then_inc(d_gf, 16)

        @block.scalar
        def _(act):
            act.dma_start(ident[:], ident_c).then_inc(d_id, 16)
            act.dma_start(rows[KB:2 * KB, 0], norm_ffn.rearrange("a (b p) -> (a b) p", p=P)).then_inc(d_nrm, 16)
            st = Steps(act, act_step)

            def split_hi(t, slot):
                act.wait_ge(d_w[slot], (t - slot) * (16 // RING) + 32)
                if not (isinstance(t, int) and t < RING):
                    act.wait_ge(mm_done, t - (RING - 1))
                n = SLOT if isinstance(t, int) and t < T_KA else TILE
                act.activation(hi[:, slot, 0:n], raw[:, slot, 0:n], ACT.Copy).then_inc(hi_done, 1)

            act.wait_ge(cst_t, 1)
            act.activation(cst[:, 0:2 * KB], pv_ps[:, 0:2 * KB], ACT.Copy).then_inc(cst_c, 1)
            act.wait_ge(cst_c, 1)
            for c in range(KB):
                act.wait_ge(x_t, c // 2 + 1)
                act.activation(act_hi[:, c], x_banks[c // 2][:, (c % 2) * S:(c % 2 + 1) * S], ACT.Copy,
                               scale=g1[:, c:c + 1]).then_inc(xhi, 1)
                if c in X_THEN:
                    split_hi(X_THEN.index(c), X_THEN.index(c))

            def rope_swap(bank, scale):
                for o in range(0, P, 32):
                    i = o ^ 32
                    ins = act.activation(swap[o:o + 32].rearrange("p a n -> p (a n)"), bank[i:i + 32, :], ACT.Copy, scale=scale)
                ins.then_inc(swap_s, 1)

            def values(bank, dst):
                act.activation(dst[:, 0], bank[:, 0:S], ACT.Copy, scale=r1c[:, 0:1])
                act.activation(dst[:, 1], bank[:, S:2 * S], ACT.Copy, scale=r1c[:, 1:2]).then_inc(evac_a, 1)

            split_hi(3, 3)
            act.wait_ge(d_x[3], 32)
            for m in range(MT):
                if m > 0:
                    st.wait()
                st.done(act.activation(flat[:, 0:D], nat[:, m, :], ACT.Square, accum_out=ss1[:, m:m + 1]))
                split_hi(4 + m, m)
            act.wait_ge(pad_s, 1)
            st.wait()
            act.activation(root1, ss1, ACT.Sqrt, bias=eps, scale=1.0 / D).then_inc(rms1_root, 1)
            split_hi(6, 2)
            for s in range(4):
                split_hi(T_KA + s + LEAD, (s + LEAD) % RING)
                if s == 0:
                    act.wait_ge(rms1_done, 1)
                    act.wait_ge(mm_done, 4)
                    for m, bank in enumerate((acc[0], acc[2])):
                        ins = act.activation(va[:, m], bank[:, 0:256], ACT.Copy, scale=r1c[:, m:m + 1])
                    ins.then_inc(evac_a, 1)
                if s == 1:
                    act.wait_ge(f_abs, 1)
                    st.done(act.activation(fg[:, 2], fg[:, 1], ACT.Exp, scale=-1.0))
                    st.wait()
                    act.activation(fg[:, 3], fg[:, 2], ACT.Ln, bias=1.0).then_inc(f_ln, 1)
                if s == 2:
                    act.wait_ge(rms1_ps, 1)
                    act.activation(r1b[:], sc_ps[:, 0, 0:S], ACT.Copy).then_inc(r1b_done, 1)
                if s == 3:
                    act.wait_ge(mm_done, T_KA + 4)
                    rope_swap(acc[1], 1.0)
                    act.wait_ge(fcum_ps, 1)
                    act.activation(fcum[:].rearrange("p a n -> p (a n)"), pv_ps[:, 0:MT * NH], ACT.Copy,
                                   scale=-1.0).then_inc(fcum_s, 1)
                    act.wait_ge(krope_s, 1)
                    for h in range(2):
                        for e in range(2):
                            act.activation(kta[h * 64:h * 64 + 64, e::2, :], rope_b[e * 64:e * 64 + 64],
                                           ACT.Copy).then_inc(kta_s, 1)

            def attention(s, slots, q):
                for p in at_slot(slots, s - 1, "S"):
                    act.wait_ge(negmax_s, q * 4 + (p + 1))
                    for t in range(2):
                        for h in range(2):
                            pr = prob[:, p, h, 0:128] if t == 0 else prob[:, p, h, 128:384]
                            ins = act.activation(pr, pr, ACT.Exp, bias=stat[:, p, 0, 2 * t + h:2 * t + h + 1],
                                                 accum_out=stat[:, p, 1, 2 * t + h:2 * t + h + 1])
                    if p < 2:
                        ins = act.activation(stat[:, p, 3], stat[:, p, 2], ACT.Exp)
                    ins.then_inc(exp_s, 1)
                for e in slots.get(s, []):
                    p = int(e[1])
                    if e[0] == "T":
                        act.wait_ge(pt_ps, q * 4 + (p + 1))
                        act.activation(prob_t[:, p % 2], tr_ps[:, :, 0:384], ACT.Copy).then_inc(pt_s, 1)
                    if e[0] == "V":
                        act.wait_ge(pv_s, q * 4 + (p + 1))
                        chunk = q * 2 + (p if p < 2 else 8 + p - 2)
                        act.activation(mix_hi[:, bass.ds(chunk, 1), :].rearrange("p a n -> p (a n)"), pv_ps[:, 0:S],
                                       ACT.Copy).then_inc(mixhi_s, 1)

            def quad(j, attend):
                for s in range(QUAD_TILES):
                    split_hi(j * QUAD_TILES + (T_QUAD + s + LEAD), (s + LEAD) % RING)
                    if s == 4:
                        act.wait_ge(mm_done, j * QUAD_TILES + (T_QUAD + 4))
                        act.wait_ge(krope_s, j + 1)
                        rope_swap(acc[0], QSCALE)
                    if s == 15:
                        act.wait_ge(mm_done, j * QUAD_TILES + (T_QUAD + 16))
                        values(acc[1], vf)
                    if attend:
                        attention(s, SLOTS_PREV, j - 1)
                    elif s == 1:
                        act.wait_ge(nft_ps, 1)
                        act.activation(nft[:], sc_ps[0:NH, 1, 0:S], ACT.Copy).then_inc(nft_s, 1)
                        act.wait_ge(cst_t, 2)
                        act.activation(cst[:, 2 * KB:384], pv_ps[:, 128:480], ACT.Copy).then_inc(cst_c, 1)
                    attention(s, SLOTS_OWN, j)

            quad(0, False)
            with act.Fori(1, QUADS) as j:
                quad(j, True)

            def take_xt(u):
                act.wait_ge(xt_ps, u + 1)
                if not (isinstance(u, int) and u == 0):
                    act.wait_ge(yt_s, u)
                act.activation(xts[:].rearrange("p a n -> p (a n)"), sc_ps[:, 0], ACT.Copy).then_inc(xts_s, 1)

            def after_y(u, par):
                act.wait_ge(yt_s, u + 1)
                if not (isinstance(u, int) and u == 0):
                    act.wait_ge(ysum_s, u)
                act.activation(ysq[:], yt[:, par], ACT.Square).then_inc(ysq_s, 1)
                for b in range(2):
                    act.activation(act_hi[:, bass.ds(u * 2 + b, 1), :].rearrange("p a n -> p (a n)"), yt[:, par, b],
                                   ACT.Copy, scale=cst[:, bass.ds(u * 2 + (KB + b), 1)]).then_inc(yhi_s, 1)

            def take_ynat(u):
                act.wait_ge(yt_ps, u + 1)
                act.activation(nat[:, :, bass.ds(u * 256, 256)], sc_ps[:, 1].rearrange("p (m n) -> p m n", m=2),
                               ACT.Copy).then_inc(ynat_s, 1)

            for s in range(4 * WOA_UNITS):
                split_hi(T_WOA + s + LEAD, (s + LEAD) % RING)
                attention(s, SLOTS_TAIL, QUADS - 1)
                if s in WOA_Y:
                    take_ynat(WOA_Y.index(s))
                if s in WOA_END:
                    after_y(WOA_END.index(s), WOA_END.index(s) % 2)
                if s in WOA_X:
                    take_xt(WOA_X.index(s))

            def wo_unit(u, par):
                t = u * 4 + (T_WOB - 4 * WOA_UNITS)
                for s in range(4):
                    split_hi(t + (s + LEAD), (s + LEAD) % RING)
                    if s == 0:
                        take_ynat(u - 1)
                    if s == 2:
                        take_xt(u)
                    if s == 3:
                        after_y(u, par)

            wo_unit(WOA_UNITS, WOA_UNITS % 2)
            with act.Fori(0, 2) as i:
                wo_unit(i * 2 + 4, 0)
                wo_unit(i * 2 + 5, 1)

            def up_step(i, first):
                for s in range(UP_TILES):
                    for t in [LEAD] if first and s == 0 else UP_SPLITS[s]:
                        split_hi(i * UP_TILES + (T_UP + t), t % RING)
                    if first and s == 0:
                        take_ynat(WO_UNITS - 1)
                    if first and s == 2:
                        act.wait_ge(y2_ps, 1)
                        act.activation(ysq[:, 0], pv_ps[:, 0:S], ACT.Sqrt, bias=eps, scale=1.0 / D).then_inc(y2_root, 1)
                    if s in (3, 7):
                        v = s // 4
                        act.wait_ge(mm_done, i * UP_TILES + (T_UP + s + 1))
                        for b in range(2):
                            act.activation(up_r[:, b], up_banks[v][b][:, S:2 * S], ACT.Copy).then_inc(upr_s, 1)
                        split_hi(i * UP_TILES + (T_UP + s + RING), s % RING)
                        for b in range(2):
                            act.wait_ge(u_s, i * 4 + (2 * v + b + 1))
                            act.activation(conv_o[:, v, b], ub[:, v, b, 2:S + 2], ACT.Identity,
                                           scale=tap(2, i * 2 + (b + v * FB)), bias=tap(3, i * 2 + (b + v * FB))).then_inc(c0_s, 1)
                    if s == 5:
                        act.wait_ge(conv_s, i * 4 + 2)
                        if not first:
                            act.wait_ge(glo_s, i)
                        act.activation(silu[:], conv_o[:, 0], ACT.Silu).then_inc(silu_s, 1)
                    if s == 7:
                        for b in range(2):
                            act.wait_ge(gated_s, i * 2 + (b + 1))
                            act.activation(g_hi[:, bass.ds(i * 2 + b, 1), :].rearrange("p a n -> p (a n)"), silu[:, b],
                                           ACT.Copy).then_inc(ghi_s, 1)

            up_step(0, True)
            with act.Fori(1, UP_STEPS) as i:
                up_step(i, False)

            def squares(n):
                if n > 0:
                    act.wait_ge(zsq_s, n)
                for m in range(MT):
                    act.wait_ge(z_s, 2 * n + (m + 5))
                    ins = act.activation(sq_out[:, m], nat[:, m, n * 512:(n + 1) * 512], ACT.Square,
                                         accum_out=ss3[:, m, n:n + 1])
                ins.then_inc(zsq_s, 1)

            for t in range(GROUPS * DOWN_TILES):
                if t == 3:
                    act.activation(small[:, 24:25], eps, ACT.Sqrt)
                if 0 < t and T_DOWN + t + LEAD < T_END:
                    split_hi(T_DOWN + t + LEAD, (t + LEAD) % RING)
                if t % DOWN_TILES == DOWN_TILES - 1 and t < LG * DOWN_TILES:
                    squares(t // DOWN_TILES)
            act.wait_ge(part_s, 1)
            for m in range(MT):
                act.wait_ge(z_s, 2 * LG + m + 5)
                act.activation(sq_out[:, m], nat[:, m, LG_COL:D], ACT.Square, accum_out=ss3[:, m, LG:GROUPS]).then_inc(zsq_s, 1)
                act.wait_ge(zsq_s, GROUPS + m)
                act.activation(root3[:, m:m + 1], ss3[:, m, LG:GROUPS], ACT.Sqrt, bias=part3[:, m:m + 1],
                               scale=1.0 / D).then_inc(z_root, 1)
                act.wait_ge(z_rms, m + GROUPS)
                act.activation(nat[:, m, 0:OUT_CUTS[1]], nat[:, m, 0:OUT_CUTS[1]], ACT.Copy,
                               scale=r3[:, m:m + 1]).then_inc(fin_a, 1)
            act.wait_ge(fin_a, 2)
            act.dma_start(out[0, P:2 * P, 0:OUT_CUTS[1]], nat[:, 1, 0:OUT_CUTS[1]]).then_inc(d_out, 16)

        @block.vector
        def _(dve):
            st = Steps(dve, dve_step)

            def split_lo(t, slot):
                dve.wait_ge(hi_done, t + 1)
                n = SLOT if isinstance(t, int) and t < T_KA else TILE
                dve.tensor_tensor(lo[:, slot, 0:n], raw[:, slot, 0:n], hi[:, slot, 0:n].bitcast(F32),
                                  ALU.subtract).then_inc(lo_done, 1)

            dve.memset(small[:, 90:91], 0.0).then_inc(read_s, 1)
            dve.memset(small[:, 91:92], 0.0).then_inc(mixlo_s, 1)
            dve.memset(small[:, 92:93], 0.0).then_inc(z_s, 4)
            dve.memset(eps, EPS).then_inc(pad_s, 1)
            dve.wait_ge(cst_c, 1)
            for c in range(KB):
                dve.wait_ge(xhi, c // 2 * 2 + 2)
                dve.scalar_tensor_tensor(act_lo[:, c], x_banks[c // 2][:, (c % 2) * S:(c % 2 + 1) * S], g1[:, c:c + 1],
                                         act_hi[:, c].bitcast(F32), ALU.mult, ALU.subtract).then_inc(xlo, 1)
                if c in X_THEN:
                    split_lo(X_THEN.index(c), X_THEN.index(c))
            split_lo(3, 3)
            dve.wait_ge(d_cst, 48)
            dve.tensor_scalar(nsink[:], nsink[:], -1.0, None, ALU.mult).then_inc(nsink_s, 1)
            split_lo(4, 0)
            split_lo(5, 1)
            dve.wait_ge(rms1_root, 1)
            dve.reciprocal(r1c, root1).then_inc(rms1_done, 1)
            dve.wait_ge(rms1_done, 1)
            dve.wait_ge(d_id, 16)
            for m in range(MT):
                dve.tensor_scalar(diag[:, m], ident[:], r1c[:, m:m + 1], None, ALU.mult).then_inc(diag_done, 1)
            split_lo(6, 2)
            dve.wait_ge(d_tab, 80)
            dve.tensor_copy(tri[:], tri_f[:]).then_inc(tri_s, 1)

            def rope(bank, scale, tmp):
                dve.scalar_tensor_tensor(tmp[:], bank[:].rearrange("p (a n) -> p a n", a=2), scale,
                                         cos_r[:].unsqueeze(1).broadcast_to([P, 2, S]), ALU.mult, ALU.mult).then_inc(evac_d, 1)

            def rope_rest(dst, tmp):
                st.done(dve.tensor_tensor(swap[:], swap[:], sin_r[:].unsqueeze(1).broadcast_to([P, 2, S]), ALU.mult))
                st.wait()
                return dve.tensor_tensor(dst[:], tmp[:], swap[:], ALU.add)

            for s in range(4):
                split_lo(T_KA + s + LEAD, (s + LEAD) % RING)
                if s == 1:
                    dve.wait_ge(evac_a, 1)
                    for m, bank in enumerate((acc[0], acc[2])):
                        st.done(dve.scalar_tensor_tensor(fg[:, 0, m], bank[:, 256:VA_COLS], r1c[:, m:m + 1],
                                                         bf_b[:], ALU.mult, ALU.add))
                    st.wait()
                    dve.scalar_tensor_tensor(fg[:, 1], fg[:, 0], -1.0, fg[:, 0], ALU.mult, ALU.max).then_inc(f_abs, 1)
                    st.done(dve.tensor_scalar(fg[:, 4], fg[:, 0], 0.0, None, ALU.min))
                    dve.wait_ge(f_ln, 1)
                    st.wait()
                    st.done(dve.tensor_tensor(fg[:, 5], fg[:, 3], fg[:, 4], ALU.subtract))
                    st.wait()
                    dve.tensor_copy(nlf_hi[:], fg[:, 5]).then_inc(nlf_s, 1)
                    dve.wait_ge(nlf_s, 1)
                    dve.tensor_tensor(nlf_lo[:], fg[:, 5], nlf_hi[:].bitcast(F32), ALU.subtract).then_inc(nlf_s, 1)
                if s == 2:
                    dve.wait_ge(r1b_done, 1)
                    st.done(dve.tensor_tensor(cos_r[:], cos_t[:], r1b[:], ALU.mult))
                    st.done(dve.tensor_tensor(sin_r[:], sin_t[:], r1b[:], ALU.mult))
                    st.wait()
                if s == 3:
                    dve.wait_ge(mm_done, T_KA + 4)
                    dve.wait_ge(swap_s, 1)
                    rope(acc[1], 1.0, rope_a)
                    dve.wait_ge(evac_d, 1)
                    rope_rest(rope_b, rope_a).then_inc(krope_s, 1)

            def attention(s, slots, q):
                for p in at_slot(slots, s - 1, "S"):
                    dve.wait_ge(exp_s, q * 4 + (p + 1))
                    if p < 2:
                        st.done(dve.tensor_tensor(stat[:, p, 1], stat[:, p, 1], stat[:, p, 3], ALU.add))
                        st.wait()
                    st.done(dve.reciprocal(stat[:, p, 4], stat[:, p, 1]))
                    st.wait()
                    for t in range(2):
                        for h in range(2):
                            pr = prob[:, p, h, 0:128] if t == 0 else prob[:, p, h, 128:384]
                            ins = dve.tensor_scalar(pr, pr, stat[:, p, 4, 2 * t + h:2 * t + h + 1], None, ALU.mult)
                    ins.then_inc(prob_s, 1)
                for e in slots.get(s, []):
                    p = int(e[1])
                    if e[0] == "S":
                        if p == 0:
                            dve.wait_ge(quad_s, q + 1)
                        if p == 2:
                            dve.wait_ge(fq_s, q + 1)
                        dve.wait_ge(scores_s, q * 4 + (p + 1))
                        if p < 2:
                            ins = dve.tensor_tensor(prob[:, p], sc_ps[:, :, 0:384],
                                                    mask_a[:].unsqueeze(1).broadcast_to([P, 2, 384]), ALU.add)
                        else:
                            dve.wait_ge(bias_s, 4)
                            bias = key_bias[:, bass.ds(q * 4, 4), :]
                            for t in range(2):
                                for h in range(2):
                                    c0, c1 = (0, 128) if t == 0 else (128, 384)
                                    i = (p - 2) * 2 + h
                                    ins = dve.scalar_tensor_tensor(prob[:, p, h, c0:c1], sc_ps[:, h, c0:c1],
                                                                   fq[:, t, i:i + 1], bias[:, i, c0:c1], ALU.add, ALU.add)
                        ins.then_inc(read_s, 1)
                        dve.wait_ge(read_s, q * 4 + (p + 2))
                        for t in range(2):
                            c0, c1 = (0, 128) if t == 0 else (128, 384)
                            ins = dve.tensor_reduce(stat[:, p, 0, 2 * t:2 * t + 2], prob[:, p, :, c0:c1], AX.X, ALU.max,
                                                    negate=True)
                            if p < 2:
                                st.done(ins)
                        if p < 2:
                            st.wait()
                            nsv = nsq[:, :, 2 * p:2 * p + 2]
                            mv = stat[:, p, 0].rearrange("p (t h) -> p t h", t=2)
                            st.done(dve.tensor_tensor(mv, mv, nsv, ALU.min))
                            st.wait()
                            ins = dve.tensor_tensor(stat[:, p, 2].rearrange("p (t h) -> p t h", t=2), mv, nsv, ALU.subtract)
                        ins.then_inc(negmax_s, 1)
                    if e[0] == "V":
                        dve.wait_ge(mixhi_s, q * 4 + (p + 1))
                        chunk = q * 2 + (p if p < 2 else 8 + p - 2)
                        mh = mix_hi[:, bass.ds(chunk, 1), :].rearrange("p a n -> p (a n)").bitcast(F32)
                        dve.tensor_tensor(mix_lo[:, bass.ds(chunk, 1), :].rearrange("p a n -> p (a n)"), pv_ps[:, 0:S], mh,
                                          ALU.subtract).then_inc(mixlo_s, 1)

            def quad(j, attend):
                for s in range(QUAD_TILES):
                    split_lo(j * QUAD_TILES + (T_QUAD + s + LEAD), (s + LEAD) % RING)
                    if s == 5:
                        dve.wait_ge(mm_done, j * QUAD_TILES + (T_QUAD + 4))
                        dve.wait_ge(swap_s, j + 2)
                        rope(acc[0], QSCALE, rope_a)
                    if s == 9:
                        dve.wait_ge(evac_d, j * 3 + 2)
                        rope_rest(qa, rope_a).then_inc(krope_s, 1)
                    if s in (8, 12):
                        dve.wait_ge(mm_done, j * QUAD_TILES + (T_QUAD + s))
                        bank, dst, scale = (acc[1], kf, 1.0) if s == 8 else (acc[0], qf, QSCALE)
                        dve.scalar_tensor_tensor(dst[:], bank[:].rearrange("p (a n) -> p a n", a=2), scale,
                                                 r1b[:].unsqueeze(1).broadcast_to([P, 2, S]), ALU.mult,
                                                 ALU.mult).then_inc(evac_d, 1)
                    if attend:
                        attention(s, SLOTS_PREV, j - 1)
                    elif s in BIAS_SLOTS:
                        n = BIAS_SLOTS.index(s)
                        dve.wait_ge(d_bias[n], 16)
                        kb = key_bias[:, 4 * n:4 * n + 4, :]
                        mask = mask_b[:].unsqueeze(1).broadcast_to([P, 4, P])
                        dve.tensor_tensor(kb[:, :, 0:P], kb[:, :, P:2 * P], mask, ALU.add)
                        dve.tensor_tensor(kb[:, :, 2 * P:384], kb[:, :, 2 * P:384], mask, ALU.add).then_inc(bias_s, 1)
                    attention(s, SLOTS_OWN, j)

            quad(0, False)
            with dve.Fori(1, QUADS) as j:
                st.loop(j, 1, QUAD_STEPS)
                quad(j, True)
                st.end(QUADS)

            def make_y(u, par, bank):
                dve.wait_ge(xts_s, u + 1)
                if not (isinstance(u, int) and u < 2):
                    dve.wait_ge(yt_ps, u - 1)
                dve.tensor_tensor(yt[:, par].rearrange("p a n -> p (a n)"), bank[:], xts[:].rearrange("p a n -> p (a n)"),
                                  ALU.add).then_inc(yt_s, 1)
                dve.wait_ge(yt_s, u + 1)
                dve.wait_ge(ysq_s, u + 1)
                if not (isinstance(u, int) and u == 0):
                    dve.wait_ge(ysum_s, u)
                dve.tensor_tensor(ysum[:], ysum[:], ysq[:], ALU.add).then_inc(ysum_s, 1)
                for b in range(2):
                    dve.wait_ge(yhi_s, u * 2 + (b + 1))
                    ins = dve.scalar_tensor_tensor(
                        act_lo[:, bass.ds(u * 2 + b, 1), :].rearrange("p a n -> p (a n)"), yt[:, par, b],
                        cst[:, bass.ds(u * 2 + (KB + b), 1)],
                        act_hi[:, bass.ds(u * 2 + b, 1), :].rearrange("p a n -> p (a n)").bitcast(F32),
                        ALU.mult, ALU.subtract)
                ins.then_inc(ylo_s, 1)

            for s in range(4 * WOA_UNITS):
                split_lo(T_WOA + s + LEAD, (s + LEAD) % RING)
                attention(s, SLOTS_TAIL, QUADS - 1)
                if s == WOA_END[0] - 1:
                    st.done(dve.memset(ysum[:], 0.0))
                    st.wait()
                if s in WOA_END:
                    u = WOA_END.index(s)
                    dve.wait_ge(mm_done, T_WOA + s + 1)
                    make_y(u, u % 2, acc[u])

            def wo_unit(u, par, bank):
                t = u * 4 + (T_WOB - 4 * WOA_UNITS)
                for s in range(4):
                    split_lo(t + (s + LEAD), (s + LEAD) % RING)
                dve.wait_ge(mm_done, t + 4)
                make_y(u, par, bank)

            wo_unit(WOA_UNITS, WOA_UNITS % 2, acc[0])
            with dve.Fori(0, 2) as i:
                wo_unit(i * 2 + 4, 0, acc[1])
                wo_unit(i * 2 + 5, 1, acc[0])

            def up_step(i, first):
                if not first:
                    st.loop(i, 1, UP_DVE_STEPS)
                for s in range(UP_TILES):
                    for t in [LEAD] if first and s == 0 else UP_SPLITS[s]:
                        split_lo(i * UP_TILES + (T_UP + t), t % RING)
                    if first and s == 2:
                        dve.wait_ge(y2_root, 1)
                        dve.reciprocal(r2b[:], ysq[:, 0]).then_inc(r2_s, 1)
                        dve.wait_ge(r2_s, 1)
                    if first and s == 1:
                        st.done(dve.memset(ub[:, :, :, 0:2], 0.0))
                        st.wait()
                    if s in (3, 7):
                        v = s // 4
                        dve.wait_ge(upr_s, i * 4 + (2 * v + 2))
                        for b in range(2):
                            st.done(dve.tensor_tensor(up_r[:, b], up_r[:, b], up_banks[v][b][:, 0:S], ALU.add))
                        st.wait()
                        for b in range(2):
                            dve.tensor_tensor(ub[:, v, b, 2:S + 2], up_r[:, b], r2b[:], ALU.mult).then_inc(u_s, 1)
                        split_lo(i * UP_TILES + (T_UP + s + RING), s % RING)
                        for b in range(2):
                            dve.wait_ge(c0_s, i * 4 + (2 * v + b + 1))
                            st.done(dve.scalar_tensor_tensor(conv_o[:, v, b], ub[:, v, b, 1:S + 1],
                                                             tap(1, i * 2 + (b + v * FB)), conv_o[:, v, b],
                                                             ALU.mult, ALU.add))
                        for b in range(2):
                            if b == 0:
                                st.wait()
                            dve.scalar_tensor_tensor(conv_o[:, v, b], ub[:, v, b, 0:S], tap(0, i * 2 + (b + v * FB)),
                                                     conv_o[:, v, b], ALU.mult, ALU.add).then_inc(conv_s, 1)
                    if s == 7:
                        dve.wait_ge(silu_s, i + 1)
                        for b in range(2):
                            dve.wait_ge(conv_s, i * 4 + (b + 3))
                            dve.tensor_tensor(silu[:, b], silu[:, b], conv_o[:, 1, b], ALU.mult).then_inc(gated_s, 1)
                        for b in range(2):
                            dve.wait_ge(ghi_s, i * 2 + (b + 1))
                            ins = dve.tensor_tensor(g_lo[:, bass.ds(i * 2 + b, 1), :].rearrange("p a n -> p (a n)"),
                                                    silu[:, b],
                                                    g_hi[:, bass.ds(i * 2 + b, 1), :].rearrange("p a n -> p (a n)").bitcast(F32),
                                                    ALU.subtract)
                        ins.then_inc(glo_s, 1)
                if not first:
                    st.end(UP_STEPS)

            up_step(0, True)
            with dve.Fori(1, UP_STEPS) as i:
                up_step(i, False)

            def make_z(n, tiles):
                bank = sc_ps if n % 2 == 0 else tr_ps
                for m in tiles:
                    dve.tensor_tensor(nat[:, m, n * 512:(n + 1) * 512], bank[:, m],
                                      nat[:, m, n * 512:(n + 1) * 512], ALU.add).then_inc(z_s, 1)

            def gain(n):
                dve.wait_ge(zsq_s, n + 1)
                for m in range(MT):
                    ins = dve.tensor_tensor(nat[:, m, n * 512:(n + 1) * 512], nat[:, m, n * 512:(n + 1) * 512],
                                            gfin[:, n * 512:(n + 1) * 512], ALU.mult)
                ins.then_inc(z_rms, 1)

            for t in range(GROUPS * DOWN_TILES):
                if 0 < t and T_DOWN + t + LEAD < T_END:
                    split_lo(T_DOWN + t + LEAD, (t + LEAD) % RING)
                n, kt = divmod(t, DOWN_TILES)
                if t == 0:
                    dve.wait_ge(ynat_s, WO_UNITS)
                if kt == DOWN_TILES - 1 and n < LG:
                    dve.wait_ge(mm_done, T_DOWN + t + 1)
                    make_z(n, range(MT))
                if kt == 4 and n > 0:
                    if n == 1:
                        dve.wait_ge(d_gf, 16)
                    gain(n - 1)
                if kt == 5 and n == LG:
                    dve.tensor_reduce(small[:, 26:28], ss3[:, :, 0:LG], AX.X, ALU.add).then_inc(z_tot, 1)
                    dve.wait_ge(z_tot, 1)
                    dve.tensor_scalar(part3, small[:, 26:28], 1.0 / D, EPS, ALU.mult, ALU.add).then_inc(part_s, 1)
            for m in range(MT):
                dve.wait_ge(last_s, m + 1)
                make_z(LG, [m])
                dve.wait_ge(z_s, 2 * LG + m + 5)
                st.done(dve.tensor_tensor(z_gain[:, m], nat[:, m, LG_COL:D], gfin[:, LG_COL:D], ALU.mult))
                dve.wait_ge(z_root, m + 1)
                dve.reciprocal(r3[:, m:m + 1], root3[:, m:m + 1]).then_inc(z_rms, 1)
                dve.wait_ge(z_rms, m + GROUPS)
                st.wait()
                for c0, c1 in zip(OUT_CUTS[1:3], OUT_CUTS[2:4]):
                    dve.tensor_scalar(nat[:, m, c0:c1], nat[:, m, c0:c1], r3[:, m:m + 1], None, ALU.mult).then_inc(fin_d, 1)
                dve.wait_ge(zsq_s, GROUPS + m)
                dve.tensor_scalar(nat[:, m, LG_COL:D], z_gain[:, m], r3[:, m:m + 1], None, ALU.mult).then_inc(fin_d, 1)

        @block.tensor
        def _(pe):
            pe.wait_ge(ones_s, 1)

            def warm(count):
                for n in range(count):
                    pe.matmul(tr_ps[:, 0, 0:P], ones[:], ones[:], start=True, stop=True)

            warm(WARM)
            pe.wait_ge(d_id, 16)

            def turn_x_pair(pr):
                pe.wait_ge(d_x[pr // 2], 32)
                if pr == 7:
                    pe.wait_ge(cst_c, 1)
                for b in range(2):
                    for m in range(MT):
                        o = b * S + m * P
                        c = 2 * pr + b
                        ins = pe.transpose(x_banks[pr][:, o:o + P], nat[:, m, c * P:(c + 1) * P], ident[:])
                ins.then_inc(x_t, 1)

            for pr in range(4):
                turn_x_pair(pr)
                if pr == 0:
                    pe.wait_ge(d_nrm, 32)
                    pe.transpose(pv_ps[:, 0:2 * KB], rows[0:2 * KB, 0, :], ident[0:2 * KB, 0:2 * KB]).then_inc(cst_t, 1)
                if pr in (1, 3):
                    warm(WARM_AGAIN[pr // 2])

            def mm3(dst, a_hi, a_lo, b_hi, b_lo, start=False):
                pe.matmul(dst, a_hi, b_hi, start=start, stop=False, skip_group_check=True)
                pe.matmul(dst, a_hi, b_lo, start=False, stop=False, skip_group_check=True)
                return pe.matmul(dst, a_lo, b_hi, start=False, stop=True, skip_group_check=True)

            def features(t, slot, bank, kt, a_hi, a_lo, first):
                pe.wait_ge(lo_done, t + 1)
                wh, wl = narrow(hi, slot), narrow(lo, slot)
                for c in range(4):
                    for b in range(2):
                        ins = mm3(bank[:, b * S:(b + 1) * S], wh[:, c, b * P:(b + 1) * P], wl[:, c, b * P:(b + 1) * P],
                                  a_hi[:, 4 * kt + c], a_lo[:, 4 * kt + c], start=first and c == 0 and b == 0)
                ins.then_inc(mm_done, 1)

            def tokens(t, slot, bank, kt, first):
                pe.wait_ge(lo_done, t + 1)
                wh, wl = narrow(hi, slot), narrow(lo, slot)
                for c in range(4):
                    for m in range(MT):
                        k = 4 * kt + c
                        ins = mm3(bank[:, m * S:(m + 1) * S], act_hi[:, k, m * P:(m + 1) * P],
                                  act_lo[:, k, m * P:(m + 1) * P], wh[:, c], wl[:, c],
                                  start=first and c == 0 and m == 0)
                ins.then_inc(mm_done, 1)

            for kt in range(4):
                pe.wait_ge(lo_done, kt + 1)
                wh, wl = with_gates(hi, kt), with_gates(lo, kt)
                for c in range(4):
                    k = 4 * kt + c
                    pe.wait_ge(xlo, k + 1 if k else 4)
                    for m, bank in enumerate((acc[0], acc[2])):
                        ins = mm3(bank[:, 0:VA_COLS], act_hi[:, k, m * P:(m + 1) * P],
                                  act_lo[:, k, m * P:(m + 1) * P], wh[:, c], wl[:, c], start=k == 0)
                ins.then_inc(mm_done, 1)
                if kt == 0:
                    for pr in range(4, 8):
                        turn_x_pair(pr)
            for kt in range(4):
                features(T_KA + kt, kt, acc[1], kt, act_hi, act_lo, kt == 0)
                if kt == 2:
                    pe.wait_ge(ones_s, 1)
                    pe.wait_ge(diag_done, 2)
                    for m in range(MT):
                        ins = pe.matmul(sc_ps[:, 0, m * P:(m + 1) * P], ones[:], diag[:, m], start=True, stop=True)
                    ins.then_inc(rms1_ps, 1)
                if kt == 3:
                    pe.wait_ge(nlf_s, 2)
                    pe.wait_ge(tri_s, 1)
                    for m in range(MT):
                        for k in range(m + 1):
                            t0 = 0 if k == m else P
                            for n, part in enumerate((nlf_hi, nlf_lo)):
                                ins = pe.matmul(pv_ps[:, m * NH:(m + 1) * NH], tri[:, t0:t0 + P], part[:, k],
                                                start=m == 0 and k == 0 and n == 0, stop=True, skip_group_check=True)
                    ins.then_inc(fcum_ps, 1)
            def attention(s, slots, q):
                for e in slots.get(s, []):
                    p = int(e[1])
                    if e[0] == "S":
                        if p == 0:
                            pe.wait_ge(quad_s, q + 1)
                            pe.wait_ge(krope_s, q + 2)
                        if p == 2:
                            pe.wait_ge(evac_d, q * 3 + 4)
                        pe.wait_ge(read_s, q * 4 + (p + 1))
                        for c0, c1, qs, n in ((0, 128, 0, 128), (128, 384, 128, 256)):
                            for h in range(2):
                                half = slice(h * HD, (h + 1) * HD)
                                qv, kv = (qa[half, p], kq[half]) if p < 2 else (qf[half, p - 2], kf[half, p - 2])
                                ins = pe.matmul(sc_ps[:, h, c0:c1], qv[:, qs:qs + 128], kv[:, 0:n], start=c0 == 0,
                                                stop=True, skip_group_check=True)
                        ins.then_inc(scores_s, 1)
                    if e[0] == "T":
                        pe.wait_ge(prob_s, q * 4 + (p + 1))
                        for h in range(2):
                            for c in range(3):
                                ins = pe.transpose(tr_ps[:, h, c * P:(c + 1) * P], prob[:, p, h, c * P:(c + 1) * P], ident[:])
                        ins.then_inc(pt_ps, 1)
                    if e[0] == "V":
                        pe.wait_ge(pt_s, q * 4 + (p + 1))
                        pe.wait_ge(mixlo_s, q * 4 + (p + 1))
                        if p == 2:
                            pe.wait_ge(evac_a, q + 2)
                        for h in range(2):
                            i = (p - 2) * 2 + h
                            v = vq[:] if p < 2 else vf[:, :, i * HD:(i + 1) * HD]
                            half = slice(h * HD, (h + 1) * HD)
                            pe.matmul(pv_ps[half, 0:S], v[:, 0], prob_t[:, p % 2, h, 0:S], start=True, stop=False,
                                      skip_group_check=True)
                            ins = pe.matmul(pv_ps[half, P:S], v[:, 1], prob_t[:, p % 2, h, S:384], start=False, stop=True,
                                            skip_group_check=True)
                        ins.then_inc(pv_s, 1)

            def quad(j, attend):
                for s in range(QUAD_TILES):
                    n, kt = divmod(s, 4)
                    if kt == 0:
                        if n == 0:
                            if attend:
                                pe.wait_ge(evac_d, j * 3 + 1)
                            else:
                                pe.wait_ge(evac_a, 1)
                        if n == 1:
                            if attend:
                                pe.wait_ge(evac_a, j + 1)
                            else:
                                pe.wait_ge(swap_s, 1)
                                pe.wait_ge(evac_d, 1)
                        if n == 2:
                            pe.wait_ge(swap_s, j + 2)
                            pe.wait_ge(evac_d, j * 3 + 2)
                        if n == 3:
                            pe.wait_ge(evac_d, j * 3 + 3)
                    t = j * QUAD_TILES + (T_QUAD + s)
                    if n < 3:
                        features(t, kt, acc[n % 2], kt, act_hi, act_lo, kt == 0)
                    else:
                        tokens(t, kt, acc[1], kt, kt == 0)
                    if attend:
                        attention(s, SLOTS_PREV, j - 1)
                    elif s == 1:
                        for n, c0, c1 in ((0, 0, S), (1, P, S)):
                            ins = pe.matmul(sc_ps[0:NH, 1, c0:c1], fg[:, 5, n], tri_f[:, 0:c1 - c0], start=n == 0,
                                            stop=n == 1, skip_group_check=True)
                        ins.then_inc(nft_ps, 1)
                        pe.wait_ge(d_cnv, 64)
                        pe.wait_ge(fcum_s, 1)
                        for k in range(4):
                            ins = pe.transpose(pv_ps[:, 128 + 88 * k:216 + 88 * k], rows[0:88, 1 + k, :], ident[0:88, 0:88])
                        ins.then_inc(cst_t, 1)
                    attention(s, SLOTS_OWN, j)

            quad(0, False)
            with pe.Fori(1, QUADS) as j:
                quad(j, True)

            def turn_x(u):
                pe.wait_ge(xcols_s, u + 1)
                for b in range(2):
                    for m in range(MT):
                        ins = pe.transpose(sc_ps[:, 0, b * S + m * P:b * S + (m + 1) * P],
                                           xcols[:, m, b * P:(b + 1) * P], ident[:])
                ins.then_inc(xt_ps, 1)

            def turn_y(u, par):
                pe.wait_ge(yt_s, u + 1)
                if not (isinstance(u, int) and u == 0):
                    pe.wait_ge(ynat_s, u)
                for m in range(MT):
                    for b in range(2):
                        ins = pe.transpose(sc_ps[:, 1, m * S + b * P:m * S + (b + 1) * P],
                                           yt[:, par, b, m * P:(m + 1) * P], ident[:])
                ins.then_inc(yt_ps, 1)

            for s, (u, kt) in enumerate(WOA_ORDER):
                if s == 0:
                    pe.wait_ge(evac_d, 3 * QUADS + 1)
                if s == 1:
                    pe.wait_ge(evac_a, QUADS + 1)
                if s == 6:
                    pe.wait_ge(mixlo_s, 4 * (QUADS - 1) + 3)
                if s == 8:
                    pe.wait_ge(mixlo_s, 4 * QUADS + 1)
                features(T_WOA + s, s % RING, acc[u], kt, mix_hi, mix_lo, kt == 0)
                attention(s, SLOTS_TAIL, QUADS - 1)
                if s in WOA_X:
                    u = WOA_X.index(s)
                    if u == 0:
                        pe.wait_ge(read_s, 4 * QUADS + 1)
                    else:
                        pe.wait_ge(xts_s, u)
                    turn_x(u)
                if s in WOA_Y:
                    turn_y(WOA_Y.index(s), WOA_Y.index(s) % 2)

            def wo_unit(u, par, bank, free):
                pe.wait_ge(yt_s, free)
                for s in range(4):
                    features(u * 4 + (T_WOB - 4 * WOA_UNITS + s), s, bank, s, mix_hi, mix_lo, s == 0)
                    if s == 0:
                        turn_y(u - 1, 1 - par)
                    if s == 2:
                        pe.wait_ge(xts_s, u)
                        turn_x(u)

            wo_unit(WOA_UNITS, WOA_UNITS % 2, acc[0], 1)
            with pe.Fori(0, 2) as i:
                wo_unit(i * 2 + 4, 0, acc[1], i * 2 + 3)
                wo_unit(i * 2 + 5, 1, acc[0], i * 2 + 4)

            def up_step(i, first):
                for s in range(UP_TILES):
                    v, kt = divmod(s, 4)
                    if kt == 0:
                        if first:
                            pe.wait_ge(yt_s, WO_UNITS - 1)
                        else:
                            pe.wait_ge(u_s, i * 4 + (2 * v - 2))
                    if first and v == 0:
                        pe.wait_ge(ylo_s, 2 * kt + 2)
                    pe.wait_ge(lo_done, i * UP_TILES + (T_UP + s + 1))
                    wh, wl = narrow(hi, kt), narrow(lo, kt)
                    for c in range(4):
                        for b in range(2):
                            k = 4 * kt + c
                            pe.matmul(up_banks[v][b].rearrange("p (a n) -> p a n", a=2), wh[:, c, b * P:(b + 1) * P],
                                      act_split[:, :, k, :], start=k == 0, stop=False, skip_group_check=True)
                            ins = pe.matmul(up_banks[v][b][:, 0:S], wl[:, c, b * P:(b + 1) * P], act_hi[:, k],
                                            start=False, stop=True, skip_group_check=True)
                    ins.then_inc(mm_done, 1)
                    if first and s == 0:
                        turn_y(WO_UNITS - 1, 1)
                    if first and s == 1:
                        pe.wait_ge(ysum_s, WO_UNITS)
                        for b in range(2):
                            ins = pe.matmul(pv_ps[:, 0:S], ones[:], ysum[:, b], start=b == 0, stop=b == 1)
                        ins.then_inc(y2_ps, 1)

            up_step(0, True)
            with pe.Fori(1, UP_STEPS) as i:
                up_step(i, False)

            pe.wait_ge(ynat_s, WO_UNITS)

            def down(n, kt, tiles):
                bank = sc_ps if n % 2 == 0 else tr_ps
                slot = (n * DOWN_TILES + kt) % RING
                wh, wl = wide(hi, slot), wide(lo, slot)
                for c in range(2):
                    for m in tiles:
                        b = 2 * kt + c
                        ins = mm3(bank[:, m], g_hi[:, b, m * P:(m + 1) * P], g_lo[:, b, m * P:(m + 1) * P],
                                  wh[:, c], wl[:, c], start=kt == 0 and c == 0)
                return ins

            for n in range(GROUPS):
                for kt in range(DOWN_TILES - (LAST if n == LG else 0)):
                    if n == 0:
                        pe.wait_ge(glo_s, kt + 1)
                    if kt == 0:
                        pe.wait_ge(z_s, 2 * n + 2)
                    pe.wait_ge(lo_done, T_DOWN + n * DOWN_TILES + kt + 1)
                    down(n, kt, range(MT)).then_inc(mm_done, 1)
            for m in range(MT):
                for kt in range(DOWN_TILES - LAST, DOWN_TILES):
                    if m == 0:
                        pe.wait_ge(lo_done, T_DOWN + LG * DOWN_TILES + kt + 1)
                    ins = down(LG, kt, [m])
                ins.then_inc(last_s, 1)


def constants():
    pos = np.arange(S)
    inv = (1.0 / (np.float32(10000.0) ** (np.arange(HD // 2, dtype=np.float32) * np.float32(2.0 / HD)))).astype(np.float32)
    ang = (pos.astype(np.float32)[None, :] * inv[:, None]).astype(np.float32)
    cos, sin = np.cos(ang).astype(np.float32), np.sin(ang).astype(np.float32)
    tri = np.triu(np.ones((P, P), np.float32))
    q, k = np.arange(P)[:, None], np.arange(S)[None, :]

    def mask(valid):
        both = np.concatenate([valid(q, k[:, :P]), valid(q + P, k)], axis=1)
        return np.where(both, 0.0, -1e30).astype(np.float32)

    return {
        "ident_c": np.eye(P, dtype=np.float32),
        "tri_c": np.concatenate([tri, np.ones((P, P), np.float32)], axis=1),
        "mask_a_c": mask(lambda q, k: (q // 64 - k // 64 >= 0) & (q // 64 - k // 64 <= 1)),
        "mask_b_c": mask(lambda q, k: k <= q)[:, :P].copy(),
        "cos_c": np.concatenate([cos] * 4),
        "sin_c": np.concatenate([-sin, sin] * 2),
    }


NAMES = ("x", "norm_mix", "w_in", "sinks", "b_f", "w_o", "norm_ffn", "w_up", "conv_w", "conv_b", "w_down", "norm_final")


def kernel(**inputs):
    import concourse.bacc as bacc
    from concourse.bass_utils import run_bass_kernel_spmd

    nc = bacc.Bacc("TRN2", target_bir_lowering=False, num_devices=1)
    arrays = {name: np.ascontiguousarray(inputs[name]) for name in NAMES}
    arrays.update(constants())
    args = [nc.dram_tensor(name, a.shape, mybir.dt.from_np(a.dtype), kind="ExternalInput").ap()
            for name, a in arrays.items()]
    result = nc.dram_tensor("result", (1, S, D), F32, kind="ExternalOutput").ap()
    program(nc, *args, result)
    return run_bass_kernel_spmd(nc, [arrays], core_ids=[0]).results[0]["result"]
```
